# Optimizing a Trainium2 kernel written in Bass

```python
import jax, jax.numpy as jnp
from jax import lax
import numpy as np

D_MODEL = 1024
BATCH = 1
SEQ = 128
DEPTH = 1
DEC_BATCH = 1
DEC_SEQ = 1024
PAST_LEN = 128

GRID_W = 64
CHUNK = 128
EPS = 1e-6
SSD_HEADS = 8
SSD_HEADDIM = 64
SSD_WIDTH = SSD_HEADS * SSD_HEADDIM
SSD_GROUPS = 2
SSD_STATE = 128
SSD_CONV = 5
XBC_DIM = SSD_WIDTH + 2 * SSD_GROUPS * SSD_STATE
RET_HEADS = 8
RET_KDIM = 64
RET_VDIM = 64
RET_QK_WIDTH = RET_HEADS * RET_KDIM
RET_V_WIDTH = RET_HEADS * RET_VDIM
ROPE_BASE = 10000.0
MIX_WIDTH = SSD_WIDTH + RET_V_WIDTH
PROJ_WIDTH = SSD_WIDTH + XBC_DIM + 2 * SSD_HEADS + 2 * RET_QK_WIDTH + 2 * RET_V_WIDTH
PEER_HEADS = 8
PEER_NKEYS = 128
PEER_EXPERTS = PEER_NKEYS * PEER_NKEYS
PEER_QDIM = 256
PEER_HALF = PEER_QDIM // 2
PEER_TOPK = 16
PEER_BLOCK = 128

kernel_name = 'hybrid_ssd_retention_peer_diffusion_step'

def rmsnorm(x, w):
    x32 = x.astype(jnp.float32)
    y = x32 * lax.rsqrt(jnp.mean(x32 * x32, axis=-1, keepdims=True) + EPS)
    return (y * w).astype(x.dtype)

def group_norm_heads(y, w, b):
    bsz, t, h, p = y.shape
    y32 = y.astype(jnp.float32)
    mu = jnp.mean(y32, axis=-1, keepdims=True)
    var = jnp.mean(jnp.square(y32 - mu), axis=-1, keepdims=True)
    yn = ((y32 - mu) * lax.rsqrt(var + EPS)).reshape(bsz, t, h * p)
    return (yn * w + b).astype(y.dtype)

def depthwise_conv_centred(x, w, bias):
    pad = SSD_CONV // 2
    y = lax.conv_general_dilated(x, w[:, None, :], window_strides=(1,), padding=[(pad, pad)],
                                 dimension_numbers=('NWC', 'WIO', 'NWC'),
                                 feature_group_count=x.shape[-1])
    return y + bias

def rope_2d(x):
    bsz, t, h, d = x.shape
    rows_n = t // GRID_W
    row = jnp.repeat(jnp.arange(rows_n), GRID_W)
    col = jnp.tile(jnp.arange(GRID_W), rows_n)
    half = d // 2
    nf = half // 2
    inv = ROPE_BASE ** (-jnp.arange(nf, dtype=jnp.float32) / nf)

    def rot(xp, pos):
        ang = pos.astype(jnp.float32)[:, None] * inv[None, :]
        cos = jnp.cos(ang)[None, :, None, :].astype(x.dtype)
        sin = jnp.sin(ang)[None, :, None, :].astype(x.dtype)
        x1, x2 = xp[..., :nf], xp[..., nf:]
        return jnp.concatenate([x1 * cos - x2 * sin, x1 * sin + x2 * cos], axis=-1)

    return jnp.concatenate([rot(x[..., :half], row), rot(x[..., half:], col)], axis=-1)

def chunk_scan(q, k, v, log_a, s0, include_diag):
    b, t, h, n = q.shape
    p = v.shape[-1]
    nc = t // CHUNK
    dt = v.dtype
    qc = q.reshape(b, nc, CHUNK, h, n)
    kc = k.reshape(b, nc, CHUNK, h, n)
    vc = v.reshape(b, nc, CHUNK, h, p)
    cum = jnp.cumsum(log_a.astype(jnp.float32).reshape(b, nc, CHUNK, h), axis=2)
    mask = jnp.tril(jnp.ones((CHUNK, CHUNK), dtype=bool), k=0 if include_diag else -1)
    seg = cum[:, :, :, None, :] - cum[:, :, None, :, :]
    decay = jnp.exp(jnp.where(mask[None, None, :, :, None], seg, -jnp.inf)).astype(dt)
    scores = jnp.einsum('bcihn,bcjhn->bcijh', qc, kc) * decay
    y_intra = jnp.einsum('bcijh,bcjhp->bcihp', scores, vc)
    w_end = jnp.exp(cum[:, :, -1:, :] - cum).astype(dt)
    chunk_states = jnp.einsum('bcjhp,bcjhn->bchpn', vc * w_end[..., None], kc)
    chunk_decay = jnp.exp(cum[:, :, -1, :]).astype(dt)

    def step(state, inp):
        st, dec = inp
        return dec[:, :, None, None] * state + st, state

    final, starts = lax.scan(step, s0.astype(dt),
                             (jnp.moveaxis(chunk_states, 1, 0), jnp.moveaxis(chunk_decay, 1, 0)))
    starts = jnp.moveaxis(starts, 0, 1)
    y_inter = jnp.einsum('bcihn,bchpn->bcihp', qc * jnp.exp(cum).astype(dt)[..., None], starts)
    return (y_intra + y_inter).reshape(b, t, h, p), final

def bidir_scan(q, k, v_f, v_b, la_f, la_b, s0_f, s0_b):
    y_f, s_f = chunk_scan(q, k, v_f, la_f, s0_f, True)
    fl = lambda a: jnp.flip(a, axis=1)
    y_b, s_b = chunk_scan(fl(q), fl(k), fl(v_b), fl(la_b), s0_b, False)
    return y_f + fl(y_b), s_f, s_b

def token_mixers(h, s0, latent, w_in, conv_w, conv_b, dt_bias_f, dt_bias_b, a_log_f, a_log_b,
                 d_skip, ssm_norm_w, ret_logit_f, ret_logit_b, ret_gn_w, ret_gn_b, w_out):
    b, t, _ = h.shape
    proj = h @ w_in
    bounds = np.cumsum([SSD_WIDTH, XBC_DIM, 2 * SSD_HEADS, RET_QK_WIDTH, RET_QK_WIDTH, RET_V_WIDTH]).tolist()
    z, xbc, dt_raw, rq, rk, rv, rg = jnp.split(proj, bounds, axis=-1)

    xbc = jax.nn.silu(depthwise_conv_centred(xbc, conv_w, conv_b))
    xs, bm, cm = jnp.split(xbc, [SSD_WIDTH, SSD_WIDTH + SSD_GROUPS * SSD_STATE], axis=-1)
    xs = xs.reshape(b, t, SSD_HEADS, SSD_HEADDIM)
    rep = SSD_HEADS // SSD_GROUPS
    bm = jnp.repeat(bm.reshape(b, t, SSD_GROUPS, SSD_STATE), rep, axis=2)
    cm = jnp.repeat(cm.reshape(b, t, SSD_GROUPS, SSD_STATE), rep, axis=2)
    dt_f = jax.nn.softplus(dt_raw[..., :SSD_HEADS] + dt_bias_f)
    dt_b = jax.nn.softplus(dt_raw[..., SSD_HEADS:] + dt_bias_b)
    y_ssd, ssd_f, ssd_b = bidir_scan(cm, bm, xs * dt_f[..., None], xs * dt_b[..., None],
                                     -dt_f * jnp.exp(a_log_f), -dt_b * jnp.exp(a_log_b), s0[0], s0[1])
    y_ssd = (y_ssd + d_skip[:, None] * xs).reshape(b, t, SSD_WIDTH)
    y_ssd = rmsnorm(y_ssd * jax.nn.silu(z), ssm_norm_w)

    q = rq.reshape(b, t, RET_HEADS, RET_KDIM)
    k = rk.reshape(b, t, RET_HEADS, RET_KDIM) * (RET_KDIM ** -0.5)
    v = rv.reshape(b, t, RET_HEADS, RET_VDIM)
    if latent:
        q = rope_2d(q)
        k = rope_2d(k)
    la_f = jnp.broadcast_to(jax.nn.log_sigmoid(ret_logit_f), (b, t, RET_HEADS))
    la_b = jnp.broadcast_to(jax.nn.log_sigmoid(ret_logit_b), (b, t, RET_HEADS))
    y_ret, ret_f, ret_b = bidir_scan(q, k, v, v, la_f, la_b, s0[2], s0[3])
    y_ret = group_norm_heads(y_ret, ret_gn_w, ret_gn_b) * jax.nn.silu(rg)

    out = jnp.concatenate([y_ssd, y_ret], axis=-1) @ w_out
    return out, (ssd_f, ssd_b, ret_f, ret_b)

def peer(h, wq, keys, u_tab, v_tab):
    b, t, d = h.shape
    q = (h @ wq).reshape(b, t, PEER_HEADS, 2, PEER_HALF)
    s = jnp.einsum('bthsd,hskd->bthsk', q, keys).astype(jnp.float32)
    s1, i1 = lax.top_k(s[..., 0, :], PEER_TOPK)
    s2, i2 = lax.top_k(s[..., 1, :], PEER_TOPK)
    cand = (s1[..., :, None] + s2[..., None, :]).reshape(b, t, PEER_HEADS, PEER_TOPK * PEER_TOPK)
    cand_idx = (i1[..., :, None] * PEER_NKEYS + i2[..., None, :]).reshape(b, t, PEER_HEADS, PEER_TOPK * PEER_TOPK)
    top, pos = lax.top_k(cand, PEER_TOPK)
    idx = jnp.take_along_axis(cand_idx, pos, axis=-1)
    g = jax.nn.softmax(top, axis=-1).astype(h.dtype)
    n_sel = PEER_HEADS * PEER_TOPK
    nb = (b * t) // PEER_BLOCK
    hb = h.reshape(nb, PEER_BLOCK, d)
    ib = idx.reshape(nb, PEER_BLOCK, n_sel)
    gb = g.reshape(nb, PEER_BLOCK, n_sel)

    def expert_block(args):
        hx, ix, gx = args
        act = jax.nn.gelu(jnp.einsum('tkd,td->tk', u_tab[ix], hx))
        return jnp.einsum('tk,tkd->td', gx * act, v_tab[ix])

    return lax.map(expert_block, (hb, ib, gb)).reshape(b, t, d)

def trunk_layer(x, mod, s0, latent, ln1_w, ln2_w, mix_w, peer_w):
    sh1, sc1, g1, sh2, sc2, g2 = jnp.split(mod, 6, axis=-1)
    h = rmsnorm(x, ln1_w) * (1 + sc1) + sh1
    mix, states = token_mixers(h, s0, latent, *mix_w)
    x = x + g1 * mix
    h = rmsnorm(x, ln2_w) * (1 + sc2) + sh2
    x = x + g2 * peer(h, *peer_w)
    return x, states

def setup_inputs(seed: int = 0) -> dict:
    key = jax.random.key(seed)
    ks = jax.random.split(key, 32)
    f32 = jnp.float32
    nrm = lambda k, shape, scale: jax.random.normal(k, shape, f32) * scale

    def dt_bias(k):
        dt = jnp.exp(jax.random.uniform(k, (DEPTH, SSD_HEADS), f32, np.log(1e-3), np.log(1e-1)))
        return dt + jnp.log(-jnp.expm1(-dt))

    hh = jnp.arange(RET_HEADS, dtype=f32)
    gamma = 1.0 - 2.0 ** (-5.0 - hh)
    base_logit = jnp.log(gamma) + (5.0 + hh) * np.float32(np.log(2.0))

    return {
        'x_prompt': nrm(ks[0], (BATCH, SEQ, D_MODEL), 1.0),
        'x_sample': nrm(ks[1], (DEC_BATCH, DEC_SEQ, D_MODEL), 1.0),
        'state_ssd_fwd': nrm(ks[2], (DEC_BATCH, DEPTH, SSD_HEADS, SSD_HEADDIM, SSD_STATE), 0.3),
        'state_ssd_bwd': nrm(ks[3], (DEC_BATCH, DEPTH, SSD_HEADS, SSD_HEADDIM, SSD_STATE), 0.3),
        'state_ret_fwd': nrm(ks[4], (DEC_BATCH, DEPTH, RET_HEADS, RET_VDIM, RET_KDIM), 0.3),
        'state_ret_bwd': nrm(ks[5], (DEC_BATCH, DEPTH, RET_HEADS, RET_VDIM, RET_KDIM), 0.3),
        'c': nrm(ks[6], (DEC_BATCH, D_MODEL), 1.0),
        'c_ctx': nrm(ks[7], (D_MODEL,), 1.0),
        'w_mod': nrm(ks[8], (DEPTH, D_MODEL, 6 * D_MODEL), 0.5 * D_MODEL ** -0.5),
        'b_mod': nrm(ks[9], (DEPTH, 6 * D_MODEL), 0.02),
        'ln1_w': 1.0 + nrm(ks[10], (DEPTH, D_MODEL), 0.05),
        'w_in': nrm(ks[11], (DEPTH, D_MODEL, PROJ_WIDTH), D_MODEL ** -0.5),
        'conv_w': nrm(ks[12], (DEPTH, SSD_CONV, XBC_DIM), SSD_CONV ** -0.5),
        'conv_b': nrm(ks[13], (DEPTH, XBC_DIM), 0.02),
        'dt_bias_f': dt_bias(ks[14]),
        'dt_bias_b': dt_bias(ks[15]),
        'a_log_f': jnp.log(jax.random.uniform(ks[16], (DEPTH, SSD_HEADS), f32, 1.0, 16.0)),
        'a_log_b': jnp.log(jax.random.uniform(ks[17], (DEPTH, SSD_HEADS), f32, 1.0, 16.0)),
        'd_skip': 1.0 + nrm(ks[18], (DEPTH, SSD_HEADS), 0.1),
        'ssm_norm_w': 1.0 + nrm(ks[19], (DEPTH, SSD_WIDTH), 0.05),
        'ret_logit_f': base_logit[None, :] + nrm(ks[20], (DEPTH, RET_HEADS), 0.1),
        'ret_logit_b': base_logit[None, :] + nrm(ks[21], (DEPTH, RET_HEADS), 0.1),
        'ret_gn_w': 1.0 + nrm(ks[22], (DEPTH, RET_V_WIDTH), 0.05),
        'ret_gn_b': nrm(ks[23], (DEPTH, RET_V_WIDTH), 0.02),
        'w_out': nrm(ks[24], (DEPTH, MIX_WIDTH, D_MODEL), MIX_WIDTH ** -0.5),
        'ln2_w': 1.0 + nrm(ks[25], (DEPTH, D_MODEL), 0.05),
        'peer_wq': nrm(ks[26], (DEPTH, D_MODEL, PEER_HEADS * PEER_QDIM), D_MODEL ** -0.5),
        'peer_keys': nrm(ks[27], (DEPTH, PEER_HEADS, 2, PEER_NKEYS, PEER_HALF), PEER_HALF ** -0.5),
        'peer_u': nrm(ks[28], (DEPTH, PEER_EXPERTS, D_MODEL), D_MODEL ** -0.5),
        'peer_v': nrm(ks[29], (DEPTH, PEER_EXPERTS, D_MODEL), 1.0),
        'lnf_w': 1.0 + nrm(ks[30], (D_MODEL,), 0.05),
    }

def reference(x_prompt, x_sample, state_ssd_fwd, state_ssd_bwd, state_ret_fwd, state_ret_bwd, c, c_ctx,
              w_mod, b_mod, ln1_w, w_in, conv_w, conv_b, dt_bias_f, dt_bias_b, a_log_f, a_log_b, d_skip,
              ssm_norm_w, ret_logit_f, ret_logit_b, ret_gn_w, ret_gn_b, w_out, ln2_w,
              peer_wq, peer_keys, peer_u, peer_v, lnf_w):
    ctx, lat = x_prompt, x_sample
    new_ssd_f, new_ssd_b, new_ret_f, new_ret_b = [], [], [], []
    for l in range(DEPTH):
        mix_w = (w_in[l], conv_w[l], conv_b[l], dt_bias_f[l], dt_bias_b[l], a_log_f[l], a_log_b[l],
                 d_skip[l], ssm_norm_w[l], ret_logit_f[l], ret_logit_b[l], ret_gn_w[l], ret_gn_b[l], w_out[l])
        peer_w = (peer_wq[l], peer_keys[l], peer_u[l], peer_v[l])
        mod_ctx = (jax.nn.silu(c_ctx) @ w_mod[l] + b_mod[l])[None, None, :]
        mod_lat = (jax.nn.silu(c) @ w_mod[l] + b_mod[l])[:, None, :]
        nb_ctx = ctx.shape[0]
        z_ssd = jnp.zeros((nb_ctx, SSD_HEADS, SSD_HEADDIM, SSD_STATE), ctx.dtype)
        z_ret = jnp.zeros((nb_ctx, RET_HEADS, RET_VDIM, RET_KDIM), ctx.dtype)
        ctx, st = trunk_layer(ctx, mod_ctx, (z_ssd, z_ssd, z_ret, z_ret), False, ln1_w[l], ln2_w[l], mix_w, peer_w)
        new_ssd_f.append(st[0])
        new_ssd_b.append(st[1])
        new_ret_f.append(st[2])
        new_ret_b.append(st[3])
        s0_lat = (state_ssd_fwd[:, l], state_ssd_bwd[:, l], state_ret_fwd[:, l], state_ret_bwd[:, l])
        lat, _ = trunk_layer(lat, mod_lat, s0_lat, True, ln1_w[l], ln2_w[l], mix_w, peer_w)
    y_prompt = rmsnorm(ctx, lnf_w)
    y_sample = rmsnorm(lat, lnf_w)
    return (y_prompt, y_sample, jnp.stack(new_ssd_f, axis=1), jnp.stack(new_ssd_b, axis=1),
            jnp.stack(new_ret_f, axis=1), jnp.stack(new_ret_b, axis=1))


_drawn_inputs = setup_inputs


def setup_inputs(seed=0):
    import zlib

    import numpy as np

    out = dict(_drawn_inputs(seed))
    spreads = {}
    factors = {'state_ssd_bwd': 3.298,
     'state_ret_fwd': 5.086,
     'state_ret_bwd': 5.045,
     'd_skip': 3.051,
     'ssm_norm_w': 3.1,
     'ret_gn_w': 3.753,
     'ret_gn_b': 17.505}
    for name, (base, spread) in spreads.items():
        noise = np.random.default_rng([zlib.crc32(name.encode()), seed]).standard_normal(out[name].shape)
        drawn = base * np.exp(spread * noise) if base else spread * noise
        out[name] = __import__('jax').numpy.asarray(drawn.astype(out[name].dtype))
    for name, factor in factors.items():
        out[name] = (out[name] * factor).astype(out[name].dtype)
    return out
```

```python
from contextlib import ExitStack

import numpy as np

import concourse.bass as bass
from concourse import mybir

F32 = mybir.dt.float32
F32R = mybir.dt.float32r
U32 = mybir.dt.uint32
ALU = mybir.AluOpType
ACT = mybir.ActivationFunctionType
AXX = mybir.AxisListType.X
UPTO = 99

P = 128
D = 1024
KD = D // P
NT = 9
T = NT * P
HEADS = 8
HD = 64
W_ = HEADS * HD
XBC = 1024
TAPS = 5
PROJ = 3600
REST0 = 512 + XBC + 16
TC = PROJ - XBC
EPS = 1e-6
NKEY = 128
TOPK = 16
NSEL = HEADS * TOPK
NEG = -1e30
LOW = -3.0e38


class Chain:

    def __init__(self, eng, sem):
        self.eng, self.sem, self.base, self.n, self.per = eng, sem, 0, 0, None

    def step(self, n):
        if isinstance(n, int) and n == 0:
            self.n = 0
            return
        if self.per is None:
            self.per = self.n
        assert self.n == self.per
        self.base, self.n = n * self.per, 0

    def link(self, ins):
        ins.then_inc(self.sem, 1)
        self.n += 1
        self.eng.wait_ge(self.sem, self.base + self.n)


class Ctx:
    pass


def new_sem(nc, ctx, name, sems):
    sems.append(ctx.enter_context(nc.semaphore(name)))
    return sems[-1]


def clear_sems(nc, sems):
    nums = sorted(s.num for s in sems)
    with nc.Block() as block:
        @block.gpsimd
        def _(pool):
            first = nums[0]
            for a, b in zip(nums, nums[1:] + [None]):
                if b != a + 1:
                    pool.sem_clear(range(first, a + 1))
                    first = b


def bcast_rows(row, n=P):
    return bass.AP(tensor=row.tensor, offset=row.offset, ap=[[0, n]] + list(row.ap)[-1:])


def modulation(nc, g):
    GW = 512
    NG = 6 * D // GW
    with ExitStack() as ctx:
        sb = lambda n, s, d=F32: ctx.enter_context(nc.sbuf_tensor(n, s, d))
        sems = []
        sem = lambda n: new_sem(nc, ctx, n, sems)
        cT, cs = sb("cT", [P, KD, 2]), sb("cs", [P, KD, 2])
        wm = [sb(f"wm{i}", [P, KD, GW]) for i in range(3)]
        bm, row = sb("bmod", [2, 6 * D]), sb("modrow", [2, 6 * D])
        lnc = sb("lnc", [P, 2, KD, 2])
        small, x_loaded, row_stored = sem("mod_small"), sem("mod_x"), sem("mod_stored")
        w_loaded = [sem(f"mod_w{i}") for i in range(3)]
        silu_done, group_done, row_done = sem("mod_silu"), sem("mod_group"), sem("mod_row")
        cols_done, chain_sem = sem("mod_cols"), sem("mod_chain")
        wv = g.w_mod.rearrange("(k p) n -> p k n", p=P)
        ctx.callback(clear_sems, nc, sems)
        block = ctx.enter_context(nc.Block())

        @block.sync
        def _(sp):
            for dst, src in ((cT[:], g.c_cols), (bm[:], g.b_mod2), (lnc[:], g.ln_cols), (g.ident[:], g.ident_d)):
                sp.dma_start(dst, src).then_inc(small, 16)
            for n in range(3):
                sp.dma_start(wm[n][:], wv[:, :, n * GW:(n + 1) * GW]).then_inc(w_loaded[n], 16)
            with sp.Fori(1, NG // 3) as i:
                for s in range(3):
                    sp.wait_ge(group_done, i * 3 + (s - 2))
                    sp.dma_start(wm[s][:], wv[:, :, bass.ds(i * (3 * GW) + s * GW, GW)]).then_inc(w_loaded[s], 16)
            sp.dma_start(g.X[:], g.x_all.rearrange("(t p) d -> p t d", p=P)).then_inc(x_loaded, 16)
            sp.wait_ge(row_done, NG + 3)
            sp.dma_start(g.mod_d, row[:]).then_inc(row_stored, 16)
            sp.wait_ge(row_stored, 16)
            sp.wait_ge(x_loaded, 16)

        @block.scalar
        def _(act):
            act.wait_ge(small, 64)
            act.activation(cs[:], cT[:], ACT.Silu).then_inc(silu_done, 1)

        @block.tensor
        def _(pe):
            pe.wait_ge(silu_done, 1)
            with pe.Fori(0, NG // 3) as i:
                for s in range(3):
                    pe.wait_ge(w_loaded[s], i * 16 + 16)
                    pe.wait_ge(row_done, i * 3 + s + 1)
                    for k in range(KD):
                        mm = pe.matmul(g.ps[s][0:2, :], cs[:, k, :], wm[s][:, k, :], start=(k == 0), stop=(k == KD - 1))
                    mm.then_inc(group_done, 1)
            pe.wait_ge(row_done, NG + 3)
            for v, col in enumerate((0, 1, 3, 4)):
                for k in range(KD):
                    c = (v * KD + k) * 2
                    mm = pe.matmul(g.ps[3][:, c:c + 2], row[0:2, col * D + k * P:col * D + (k + 1) * P],
                                   g.ident[0:2, 0:2], start=True, stop=True)
            mm.then_inc(cols_done, 1)

        @block.vector
        def _(dve):
            own = Chain(dve, chain_sem)
            dve.sem_inc(row_done, 3)
            dve.wait_ge(small, 64)
            with dve.Fori(0, NG // 3) as i:
                for s in range(3):
                    dve.wait_ge(group_done, i * 3 + s + 1)
                    cols = bass.ds(i * (3 * GW) + s * GW, GW)
                    dve.tensor_tensor(row[:, cols], g.ps[s][0:2, :], bm[:, cols], ALU.add).then_inc(row_done, 1)
            dve.wait_ge(cols_done, 1)
            m = g.ps[3][:, 0:4 * KD * 2].rearrange("p (v k s) -> p v k s", v=4, k=KD)
            for v in range(2):
                own.link(dve.tensor_copy(g.shift[:, v], m[:, 2 * v]))
                own.link(dve.scalar_tensor_tensor(g.gain[:, v], m[:, 2 * v + 1], 1.0, lnc[:, v], ALU.add, ALU.mult))


def norm_transpose(nc, g, v):
    with ExitStack() as ctx:
        sb = lambda n, s, d=F32: ctx.enter_context(nc.sbuf_tensor(n, s, d))
        sems = []
        sem = lambda n: new_sem(nc, ctx, f"nt{v}_{n}", sems)
        xn = [sb(f"xn{v}{i}", [P, D]) for i in range(2)]
        junk = sb(f"ntjunk{v}", [P, D])
        ss, rs = sb(f"ntss{v}", [P, NT]), sb(f"ntrs{v}", [P, NT])
        chain_sem, ms_ready, root_done, rstd_ready = sem("chain"), sem("ms"), sem("root"), sem("rstd")
        xn_ready, xn_free, turned, banks_free_a, banks_free_v = (
            sem("xn"), sem("xnfree"), sem("turned"), sem("bfa"), sem("bfv"))
        ctx.callback(clear_sems, nc, sems)
        block = ctx.enter_context(nc.Block())
        H = KD // 2
        x_loaded = sem("x")

        @block.sync
        def _(sp):
            if v == 1:
                sp.dma_start(g.X[:], g.x1_d.rearrange("(t p) d -> p t d", p=P)).then_inc(x_loaded, 16)

        def tiles(eng, body):
            body(0, 0, 0)
            with eng.Fori(0, (NT - 1) // 2) as i:
                body(i * 2 + 1, 1, 1)
                body(i * 2 + 2, 0, 1)

        @block.scalar
        def _(act):
            act.sem_inc(banks_free_a, 2)
            act.wait_ge(ms_ready, 1)
            act.activation(rs[:], ss[:], ACT.Sqrt).then_inc(root_done, 1)

            def body(t, s, seq):
                act.wait_ge(turned, t + 1)
                for k in range(H):
                    a = act.activation(g.hT[:, k, bass.ds(t * P, P)], g.ps[4 * s + k // 4][:, (k % 4) * P:(k % 4 + 1) * P],
                                       ACT.Identity, bias=g.shift[:, v, k, seq:seq + 1], scale=g.gain[:, v, k, seq:seq + 1])
                a.then_inc(banks_free_a, 1)
            tiles(act, body)

        @block.vector
        def _(dve):
            own = Chain(dve, chain_sem)
            dve.sem_inc(banks_free_v, 2)
            if v == 1:
                dve.wait_ge(x_loaded, 16)
            for t in range(NT):
                own.link(dve.tensor_tensor_reduce(junk[:], g.X[:, t, :], g.X[:, t, :], 1.0, 0.0, ALU.mult, ALU.add,
                                                  ss[:, t:t + 1]))
            own.link(dve.tensor_scalar(ss[:], ss[:], 1.0 / D, EPS, ALU.mult, ALU.add))
            dve.sem_inc(ms_ready, 1)
            dve.wait_ge(root_done, 1)
            own.link(dve.reciprocal(rs[:], rs[:]))

            def scale(t, s):
                dve.wait_ge(xn_free, t + 1)
                dve.tensor_scalar(xn[s][:], g.X[:, t, :], rs[:, bass.ds(t, 1)], None, ALU.mult).then_inc(xn_ready, 1)

            def evac(t, s, seq):
                dve.wait_ge(turned, t + 1)
                for k in range(H, KD):
                    a = dve.tensor_scalar(g.hT[:, k, bass.ds(t * P, P)], g.ps[4 * s + k // 4][:, (k % 4) * P:(k % 4 + 1) * P],
                                          g.gain[:, v, k, seq:seq + 1], g.shift[:, v, k, seq:seq + 1], ALU.mult, ALU.add)
                a.then_inc(banks_free_v, 1)

            scale(0, 0)
            scale(1, 1)
            evac(0, 0, 0)
            with dve.Fori(0, (NT - 1) // 2 - 1) as i:
                scale(i * 2 + 2, 0)
                evac(i * 2 + 1, 1, 1)
                scale(i * 2 + 3, 1)
                evac(i * 2 + 2, 0, 1)
            scale(NT - 1, 0)
            evac(NT - 2, 1, 1)
            evac(NT - 1, 0, 1)

        @block.tensor
        def _(pe):
            pe.sem_inc(xn_free, 2)

            def body(t, s, seq):
                pe.wait_ge(xn_ready, t + 1)
                pe.wait_ge(banks_free_a, t + 1)
                pe.wait_ge(banks_free_v, t + 1)
                for k in range(KD):
                    mm = pe.transpose(g.ps[4 * s + k // 4][:, (k % 4) * P:(k % 4 + 1) * P], xn[s][:, k * P:(k + 1) * P],
                                      g.ident[:])
                mm.then_inc(turned, 1)
                pe.wait_ge(turned, t + 1)
                pe.sem_inc(xn_free, 1)
            tiles(pe, body)


def project_in(nc, g):
    PAD = TAPS // 2
    WID = T + 4 * PAD
    LAT = P + 2 * PAD
    TG = 384
    NB = XBC // P
    NQ = 3
    with ExitStack() as ctx:
        sb = lambda n, s, d=F32: ctx.enter_context(nc.sbuf_tensor(n, s, d))
        sems = []
        sem = lambda n: new_sem(nc, ctx, f"pi_{n}", sems)
        wx = [sb(f"wx{i}", [P, KD, P]) for i in range(2)]
        pre = [sb(f"pre{i}", [P, WID]) for i in range(2)]
        acc = [sb(f"acc{i}", [P, WID - 2 * PAD]) for i in range(2)]
        cv = [sb(f"cv{i}", [P, T]) for i in range(2)]
        cw, cb = sb("cw", [P, NB, TAPS]), sb("cb", [P, NB])
        wt = [sb(f"wt{i}", [P, KD, 512]) for i in range(2)]
        wd, dts = sb("wdt", [P, KD, 16]), sb("dts", [P, NT, 16])
        st = [sb(f"st{i}", [P, 512]) for i in range(NQ)]
        small, wd_loaded, padded, chain_sem, chain_sem_v = sem("small"), sem("wd"), sem("padded"), sem("chain"), sem("chainv")
        wx_loaded, wt_loaded = [sem("wx0"), sem("wx1")], [sem("wt0"), sem("wt1")]
        block_done, banks_free, pre_ready, pre_free = sem("block"), sem("banksfree"), sem("pre"), sem("prefree")
        conv_done, acc_free, silu_done = sem("conv"), sem("accfree"), sem("silu")
        cv_stored = [sem("cvst0"), sem("cvst1")]
        dt_done, dt_copied, dt_stored = sem("dt"), sem("dtcopied"), sem("dtstored")
        tile_done, tile_copied, group_done = sem("tile"), sem("tilecopied"), sem("group")
        st_stored = [sem(f"st{i}") for i in range(NQ)]
        wv = g.w_in.rearrange("(k p) n -> p k n", p=P)
        ctx.callback(clear_sems, nc, sems)
        block = ctx.enter_context(nc.Block())

        def groups(eng, body):
            body(0, 0)
            with eng.Fori(0, 2) as i:
                body(i * 2 + 1, 1)
                body(i * 2 + 2, 0)

        @block.gpsimd
        def _(pool):
            for s in range(2):
                for a, b in ((0, PAD), (PAD + P, 3 * PAD + P), (WID - PAD, WID)):
                    pool.memset(pre[s][:, a:b], 0.0).then_inc(padded, 1)
            pool.dma_start(cw[:], g.conv_w_cols).then_inc(small, 16)
            pool.dma_start(cb[:], g.conv_b_cols).then_inc(small, 16)
            for s in range(2):
                pool.dma_start(wx[s][:], wv[:, :, 512 + s * P:512 + (s + 1) * P]).then_inc(wx_loaded[s], 16)
            pool.dma_start(wd[:], wv[:, :, 512 + XBC:REST0]).then_inc(wd_loaded, 16)
            pool.dma_start(wt[0][:], wv[:, :, 0:512]).then_inc(wt_loaded[0], 16)
            pool.dma_start(wt[1][:], wv[:, :, REST0:REST0 + 512]).then_inc(wt_loaded[1], 16)
            with pool.Fori(0, NB // 2 - 1) as i:
                for s in range(2):
                    pool.wait_ge(block_done, i * 2 + s + 1)
                    pool.dma_start(wx[s][:], wv[:, :, bass.ds(i * (2 * P) + (512 + (2 + s) * P), P)]).then_inc(wx_loaded[s], 16)
            for j in range(3):
                pool.wait_ge(group_done, j + 1)
                c = REST0 + (j + 1) * 512
                pool.dma_start(wt[j % 2][:], wv[:, :, c:c + 512]).then_inc(wt_loaded[j % 2], 16)

        @block.sync
        def _(sp):
            for s in range(2):
                sp.sem_inc(cv_stored[s], 16)
            for s in range(NQ):
                sp.sem_inc(st_stored[s], 16)
            with sp.Fori(0, NB // 2) as i:
                for s in range(2):
                    sp.wait_ge(silu_done, i * 2 + s + 1)
                    sp.dma_start(g.xbc_d[bass.ds(i * (2 * P) + s * P, P), :], cv[s][:]).then_inc(cv_stored[s], 16)
            sp.wait_ge(dt_copied, 1)
            sp.dma_start(g.tok_d[:, 5 * 512:].rearrange("(t p) c -> p t c", p=P), dts[:]).then_inc(dt_stored, 16)

            def store(grp, s):
                for t in range(NT):
                    sp.wait_ge(tile_copied, grp * NT + t + 1)
                    sp.dma_start(g.tok_d[t * P:(t + 1) * P, bass.ds(grp * 512, 512)], st[t % NQ][:]).then_inc(st_stored[t % NQ], 16)
            groups(sp, store)
            for s in range(2):
                sp.wait_ge(cv_stored[s], 16 * (NB // 2 + 1))
            sp.wait_ge(dt_stored, 16)
            for s in range(NQ):
                sp.wait_ge(st_stored[s], 16 * (5 * NT // NQ + 1))

        @block.tensor
        def _(pe):
            with pe.Fori(0, NB // 2) as i:
                for s in range(2):
                    pe.wait_ge(wx_loaded[s], i * 16 + 16)
                    pe.wait_ge(banks_free, i * 2 + s + 1)
                    for q in range(T // TG):
                        for k in range(KD):
                            mm = pe.matmul(g.ps[3 * s + q][:, 0:TG], wx[s][:, k, :], g.hT[:, k, q * TG:(q + 1) * TG],
                                           start=(k == 0), stop=(k == KD - 1))
                    mm.then_inc(block_done, 1)
            pe.wait_ge(wd_loaded, 16)
            for t in range(NT):
                for k in range(KD):
                    mm = pe.matmul(g.ps[6][:, 16 * t:16 * t + 16], g.hT[:, k, t * P:(t + 1) * P], wd[:, k, :],
                                   start=(k == 0), stop=(k == KD - 1))
            mm.then_inc(dt_done, 1)
            pe.wait_ge(banks_free, NB + 2)

            def group(grp, s):
                pe.wait_ge(wt_loaded[s], (grp // 2) * 16 + 16)
                for t in range(NT):
                    if not (isinstance(grp, int) and t < NQ):
                        pe.wait_ge(tile_copied, grp * NT + (t - NQ + 1))
                    for k in range(KD):
                        mm = pe.matmul(g.ps[t % NQ][:], g.hT[:, k, t * P:(t + 1) * P], wt[s][:, k, :],
                                       start=(k == 0), stop=(k == KD - 1))
                    mm.then_inc(tile_done, 1)
                pe.wait_ge(tile_done, grp * NT + NT)
                pe.sem_inc(group_done, 1)
            groups(pe, group)

        @block.scalar
        def _(act):
            act.sem_inc(banks_free, 2)
            act.wait_ge(padded, 6)
            act.wait_ge(small, 32)

            def copy_in(n, s, i):
                act.wait_ge(block_done, n + 1)
                act.wait_ge(pre_free, n + 1)
                act.activation(pre[s][:, PAD:PAD + P], g.ps[3 * s][:, 0:P], ACT.Copy)
                act.activation(pre[s][:, 3 * PAD + P:3 * PAD + TG], g.ps[3 * s][:, P:TG], ACT.Copy)
                for q in range(1, T // TG):
                    z = act.activation(pre[s][:, 3 * PAD + q * TG:3 * PAD + (q + 1) * TG], g.ps[3 * s + q][:, 0:TG], ACT.Copy)
                z.then_inc(pre_ready, 1)
                act.wait_ge(pre_ready, n + 1)
                act.sem_inc(banks_free, 1)

            def silu(n, s, i):
                act.wait_ge(conv_done, n + 1)
                act.wait_ge(cv_stored[s], i * 16 + 16)
                act.activation(cv[s][:, 0:P], acc[s][:, 0:P], ACT.Silu, bias=cb[:, bass.ds(n, 1)]).then_inc(chain_sem, 1)
                act.activation(cv[s][:, P:T], acc[s][:, LAT:LAT + T - P], ACT.Silu, bias=cb[:, bass.ds(n, 1)]).then_inc(chain_sem, 1)
                act.wait_ge(chain_sem, n * 2 + 2)
                act.sem_inc(silu_done, 1)
                act.sem_inc(acc_free, 1)
            with act.Fori(0, NB // 2) as i:
                for s in range(2):
                    copy_in(i * 2 + s, s, i)
                    silu(i * 2 + s, s, i)
            act.wait_ge(dt_done, 1)
            act.activation(dts[:], g.ps[6][:, 0:16 * NT].rearrange("p (t c) -> p t c", t=NT), ACT.Copy).then_inc(dt_copied, 1)

            def group(grp, s):
                for t in range(NT):
                    act.wait_ge(tile_done, grp * NT + t + 1)
                    act.wait_ge(st_stored[t % NQ], grp * (16 * NT // NQ) + (t // NQ) * 16 + 16)
                    act.activation(st[t % NQ][:], g.ps[t % NQ][:], ACT.Copy).then_inc(tile_copied, 1)
            groups(act, group)

        @block.vector
        def _(dve):
            dve.sem_inc(pre_free, 2)
            dve.sem_inc(acc_free, 2)
            dve.wait_ge(small, 32)
            with dve.Fori(0, NB // 2) as i:
                for s in range(2):
                    n = i * 2 + s
                    dve.wait_ge(pre_ready, n + 1)
                    dve.wait_ge(acc_free, n + 1)
                    N = WID - 2 * PAD
                    for tap in range(TAPS):
                        w = cw[:, bass.ds(n, 1), tap]
                        x = pre[s][:, tap:tap + N]
                        if tap == 0:
                            z = dve.tensor_scalar(acc[s][:], x, w, None, ALU.mult)
                        else:
                            z = dve.scalar_tensor_tensor(acc[s][:], x, w, acc[s][:], ALU.mult, ALU.add)
                        z.then_inc(chain_sem_v, 1)
                        dve.wait_ge(chain_sem_v, n * TAPS + tap + 1)
                    dve.sem_inc(conv_done, 1)
                    dve.sem_inc(pre_free, 1)


NR = NT + 1
RSC = HD ** -0.5


def decay_terms(nc, g):
    with ExitStack() as ctx:
        sb = lambda n, s, d=F32: ctx.enter_context(nc.sbuf_tensor(n, s, d))
        sems = []
        sem = lambda n: new_sem(nc, ctx, f"dc_{n}", sems)
        x, u, w, l, c, m = (sb(f"dc{n}", [P, NR, 16]) for n in "xuwlcm")
        bias, alog, la = sb("dcbias", [P, 16]), sb("dcalog", [P, 16]), sb("dcla", [P, NR, 16])
        cum, tri = sb("cum", [P, NR, 16]), sb("tri", [P, 3, P])
        ef, eb = sb("ef", [P, HEADS, P]), sb("eb", [P, HEADS, P])
        loaded, x_ready, u_ready, w_ready, l_ready, a_ready = (sem(n) for n in ("ld", "x", "u", "w", "l", "a"))
        la_ready, sums_done, cum_ready, exps_done, turned, cumT_ready, seg_done, seg_exp = (
            sem(n) for n in ("la", "sums", "cum", "exps", "turned", "cumT", "seg", "segexp"))
        chain = sem("chain")
        ctx.callback(clear_sems, nc, sems)
        block = ctx.enter_context(nc.Block())

        @block.sync
        def _(sp):
            for dst, src in ((x[:, 0:NT, :], g.tok_d[:, 5 * 512:].rearrange("(t p) c -> p t c", p=P)),
                             (x[:, NT, :], g.ret_logits), (bias[:], g.dt_biases), (alog[:], g.a_logs),
                             (tri[:], g.tri_d), (g.sel[:], g.sel_d), (g.mneg[:], g.mneg_d)):
                sp.dma_start(dst, src).then_inc(loaded, 16)

        @block.scalar
        def _(act):
            act.wait_ge(loaded, 7 * 16)
            act.activation(alog[:], alog[:], ACT.Exp).then_inc(a_ready, 1)
            act.wait_ge(x_ready, 1)
            act.activation(u[:], m[:], ACT.Exp).then_inc(u_ready, 1)
            act.wait_ge(w_ready, 1)
            act.activation(l[:], w[:], ACT.Ln).then_inc(l_ready, 1)
            act.wait_ge(cum_ready, 1)
            act.activation(g.EC[:], cum[:], ACT.Exp).then_inc(exps_done, 1)
            act.activation(g.WD[:], c[:], ACT.Exp).then_inc(exps_done, 1)
            act.activation(g.CD[:], g.ps[2][:, 0:16 * NR].rearrange("p (r c) -> p r c", r=NR), ACT.Exp).then_inc(exps_done, 1)
            act.wait_ge(turned, 1)
            for r in range(NR):
                z = act.activation(g.cumT[:, r * P:(r + 1) * P], g.ps[4 + r // 4][0:16, (r % 4) * P:(r % 4 + 1) * P], ACT.Copy)
            z.then_inc(cumT_ready, 1)
            act.wait_ge(seg_done, 1)
            for h in range(16):
                e = ef if h < 8 else eb
                z = act.activation(e[:, h % 8, :], g.ps[h // 4][:, (h % 4) * P:(h % 4 + 1) * P], ACT.Exp,
                                   bias=g.NC[:, NT, h:h + 1])
            z.then_inc(seg_exp, 1)

        @block.vector
        def _(dve):
            own = Chain(dve, chain)
            dve.wait_ge(loaded, 7 * 16)
            own.link(dve.tensor_tensor(x[:, 0:NT], x[:, 0:NT], bias[:].unsqueeze(1).broadcast_to([P, NT, 16]), ALU.add))
            own.link(dve.tensor_scalar(x[:, NT], x[:, NT], -1.0, None, ALU.mult))
            own.link(dve.scalar_tensor_tensor(m[:], x[:], -1.0, x[:], ALU.mult, ALU.min))
            dve.sem_inc(x_ready, 1)
            dve.wait_ge(u_ready, 1)
            own.link(dve.tensor_scalar(w[:], u[:], 1.0, None, ALU.add))
            dve.sem_inc(w_ready, 1)
            own.link(dve.tensor_scalar(c[:], w[:], 1.0, None, ALU.subtract))
            own.link(dve.scalar_tensor_tensor(m[:], c[:], 0.0, u[:], ALU.is_equal, ALU.mult))
            own.link(dve.tensor_scalar(c[:], c[:], 1e-30, None, ALU.max))
            own.link(dve.reciprocal(c[:], c[:]))
            own.link(dve.tensor_tensor(c[:], c[:], u[:], ALU.mult))
            dve.wait_ge(l_ready, 1)
            own.link(dve.tensor_tensor(c[:], c[:], l[:], ALU.mult))
            own.link(dve.tensor_tensor(c[:], c[:], m[:], ALU.add))
            own.link(dve.scalar_tensor_tensor(g.DT[:], x[:], 0.0, c[:], ALU.max, ALU.add))
            dve.wait_ge(a_ready, 1)
            own.link(dve.tensor_tensor(la[:, 0:NT], g.DT[:, 0:NT], alog[:].unsqueeze(1).broadcast_to([P, NT, 16]), ALU.mult))
            own.link(dve.tensor_scalar(la[:, 0:NT], la[:, 0:NT], -1.0, None, ALU.mult))
            own.link(dve.tensor_scalar(la[:, NT], g.DT[:, NT], -1.0, None, ALU.mult))
            dve.sem_inc(la_ready, 1)
            dve.wait_ge(sums_done, 1)
            for d in range(2):
                own.link(dve.tensor_copy(cum[:, :, 8 * d:8 * d + 8], g.ps[d][:, 0:8 * NR].rearrange("p (r c) -> p r c", r=NR)))
            own.link(dve.tensor_scalar(g.NC[:], cum[:], -1.0, None, ALU.mult))
            own.link(dve.tensor_tensor(c[:], g.ps[2][:, 0:16 * NR].rearrange("p (r c) -> p r c", r=NR), cum[:], ALU.subtract))
            dve.sem_inc(cum_ready, 1)
            dve.wait_ge(exps_done, 3)
            own.link(dve.tensor_tensor(g.WD[:, 0:NT], g.WD[:, 0:NT], g.DT[:, 0:NT], ALU.mult))
            own.link(dve.tensor_scalar(g.WD[:, NT], g.WD[:, NT], RSC, None, ALU.mult))
            dve.wait_ge(seg_exp, 1)
            own.link(dve.tensor_tensor(ef[:], ef[:], eb[:], ALU.add))
            own.link(dve.tensor_scalar(g.Dret[:], ef[:], RSC, None, ALU.mult))

        @block.tensor
        def _(pe):
            pe.wait_ge(la_ready, 1)
            pe.matmul(g.ps[0][:, 0:8 * NR], tri[:, 0, :], la[:, :, 0:8], start=True, stop=True)
            pe.matmul(g.ps[1][:, 0:8 * NR], tri[:, 1, :], la[:, :, 8:16], start=True, stop=True)
            pe.matmul(g.ps[2][:, 0:16 * NR], tri[:, 2, :], la[:], start=True, stop=True).then_inc(sums_done, 1)
            pe.wait_ge(cum_ready, 1)
            for r in range(NR):
                mm = pe.transpose(g.ps[4 + r // 4][0:16, (r % 4) * P:(r % 4 + 1) * P], cum[:, r, :], g.ident[:])
            mm.then_inc(turned, 1)
            pe.wait_ge(cumT_ready, 1)
            pe.wait_ge(exps_done, 3)
            seg = None
            for q in range(4):
                seg = segment(pe, g, q, g.ps[q], NT)
            seg.then_inc(seg_done, 1)


def segment(pe, g, q, bank, r):
    mm = pe.matmul(bank[:], g.ident[:], g.mneg[:, q // 2], start=True, stop=False, skip_group_check=True)
    for h in range(4):
        mm = pe.matmul(bank[:, h * P:(h + 1) * P], g.sel[:, 4 * q + h, :], g.cumT[:, bass.ds(r * P, P)],
                       start=False, stop=(h == 3), skip_group_check=True)
    return mm


def heads_bcast(ap):
    return ap.unsqueeze(2).broadcast_to([ap.shape[0], HEADS, HD])


REC = W_ + 2 * P + 2 * W_


def backward_states(nc, g):
    with ExitStack() as ctx:
        sb = lambda n, s, d=F32: ctx.enter_context(nc.sbuf_tensor(n, s, d))
        sems = []
        sem = lambda n: new_sem(nc, ctx, f"bw_{n}", sems)
        tk = [sb(f"bwtk{i}", [P, 3 * W_]) for i in range(2)]
        xb = [sb(f"bwxb{i}", [P, 6, P]) for i in range(2)]
        rec = [sb(f"bwrec{i}", [P, REC]) for i in range(2)]
        rt, rp = sb("bwrt", [P, 2 * W_]), sb("bwrp", [P, 2 * W_])
        rope = sb("rope", [P, NT, 96])
        xw, vw = sb("bwxw", [P, W_]), sb("bwvw", [P, W_])
        tmp, tmpr = sb("bwtmp", [P, W_]), sb("bwtmpr", [HD, W_])
        small, zeroed, loaded = sem("small"), sem("zeroed"), [sem("ld0"), sem("ld1")]
        turned, x_copied, k_ready, xw_ready, vw_ready, states_done, state_ready = (
            sem(n) for n in ("turned", "xcopied", "k", "xw", "vw", "states", "state"))
        rec_stored, out_stored, chain = [sem("rec0"), sem("rec1")], sem("out"), sem("chain")
        ctx.callback(clear_sems, nc, sems)
        block = ctx.enter_context(nc.Block())

        def steps(eng, body):
            body(0, 0, 0, 0, 1)
            with eng.Fori(0, (NT - 1) // 2) as i:
                for s in (1, 0):
                    tile = eng.snap(i * -2 + (7 + s))
                    body(i * 2 + (2 - s), s, tile, tile + 1, tile)

        @block.sync
        def _(sp):
            sp.dma_start(rope[:], g.rope_d.rearrange("(t p) c -> p t c", p=P)).then_inc(small, 16)
            sp.dma_start(g.SB[:, NT, :], g.ssd_bwd_T).then_inc(small, 16)
            sp.dma_start(g.SBr[:, NT, :], g.ret_bwd_T).then_inc(small, 16)
            sp.sem_inc(rec_stored[0], 16)
            sp.sem_inc(rec_stored[1], 16)
            sp.sem_inc(state_ready, 2)

            def load(n, s, t, a, b):
                sp.wait_ge(state_ready, n + 1)
                rows = bass.ds(t * P, P)
                sp.dma_start(tk[s][:], g.tok_d[rows, W_:4 * W_]).then_inc(loaded[s], 16)
                sp.dma_start(xb[s][:], g.xbc_d[0:6 * P, :].rearrange("(c p) t -> p c t", p=P)[:, :, rows]).then_inc(loaded[s], 16)
            steps(sp, load)

        @block.scalar
        def _(act):
            def copy(n, s, t, a, b):
                act.wait_ge(turned, n + 1)
                act.wait_ge(rec_stored[s], ((n // 2) * 16 + 16))
                act.activation(rec[s][:, 0:W_], g.ps[0][:], ACT.Copy)
                act.activation(rec[s][:, W_:W_ + 2 * P], g.ps[1][:, 0:2 * P], ACT.Copy).then_inc(x_copied, 1)
                act.wait_ge(x_copied, n + 1)
                act.wait_ge(k_ready, n + 1)
                act.dma_start(g.rec_d[bass.ds(t * P, P), :], rec[s][:]).then_inc(rec_stored[s], 16)
                if isinstance(n, int):
                    act.wait_ge(state_ready, n + 3)
                    act.dma_start(g.ssd_b_out, g.SB[:, b, :]).then_inc(out_stored, 16)
                    act.dma_start(g.ret_b_out, g.SBr[:, b, :]).then_inc(out_stored, 16)
            steps(act, copy)
            act.wait_ge(out_stored, 32)
            act.wait_ge(rec_stored[0], 16 * 6)
            act.wait_ge(rec_stored[1], 16 * 5)

        @block.gpsimd
        def _(pool):
            pool.memset(g.SB[:, 0, :], 0.0).then_inc(zeroed, 1)
            pool.memset(g.SBr[:, 0, :], 0.0).then_inc(zeroed, 1)

            def weigh(n, s, t, a, b):
                pool.wait_ge(loaded[s], (n // 2) * 32 + 32)
                pool.wait_ge(state_ready, n + 2)
                pool.tensor_tensor(vw[:].rearrange("p (h d) -> p h d", h=HEADS), tk[s][:, 2 * W_:].rearrange("p (h d) -> p h d", h=HEADS),
                                   heads_bcast(g.WD[:, NT, 8:16]), ALU.mult).then_inc(vw_ready, 1)
            steps(pool, weigh)

        @block.vector
        def _(dve):
            own = Chain(dve, chain)
            dve.wait_ge(small, 48)
            dve.wait_ge(zeroed, 2)

            def step(n, s, t, a, b):
                own.step(n)
                dve.wait_ge(loaded[s], (n // 2) * 32 + 32)
                dve.wait_ge(rec_stored[s], (n // 2) * 16 + 16)
                qk = tk[s][:, 0:2 * W_]
                v4 = lambda ap, i: ap.rearrange("p (h f i c) -> p h f i c", f=2, i=2, c=16)[:, :, :, i, :]
                sin = rope[:, bass.ds(t, 1), 64:96].rearrange("p o (f c) -> p (o f) c", f=2).unsqueeze(1).broadcast_to([P, 16, 2, 16])
                dve.tensor_tensor(rp[:].rearrange("p (h c) -> p h c", c=HD), qk.rearrange("p (h c) -> p h c", c=HD),
                                  rope[:, bass.ds(t, 1), 0:64].broadcast_to([P, 16, HD]), ALU.mult)
                own.link(dve.tensor_tensor(v4(rt[:], 0), v4(qk, 1), sin, ALU.mult))
                own.link(dve.tensor_tensor(v4(rt[:], 1), v4(qk, 0), sin, ALU.mult))
                out = rec[s][:, W_ + 2 * P:REC]
                own.link(dve.tensor_tensor(v4(out, 0), v4(rp[:], 0), v4(rt[:], 0), ALU.subtract))
                own.link(dve.tensor_tensor(v4(out, 1), v4(rp[:], 1), v4(rt[:], 1), ALU.add))
                dve.sem_inc(k_ready, 1)
                dve.wait_ge(x_copied, n + 1)
                dve.tensor_tensor(xw[:].rearrange("p (h d) -> p h d", h=HEADS), rec[s][:, 0:W_].rearrange("p (h d) -> p h d", h=HEADS),
                                  g.WD[:, bass.ds(t, 1), 8:16].rearrange("p o h -> p (o h)").unsqueeze(2).broadcast_to([P, HEADS, HD]),
                                  ALU.mult).then_inc(xw_ready, 1)
                own.link(dve.tensor_tensor(tmp[:].rearrange("p (h d) -> p h d", h=HEADS),
                                           g.SB[:, bass.ds(a, 1), :].rearrange("p o (h d) -> p (o h) d", h=HEADS),
                                           g.CD[:, bass.ds(t, 1), 8:16].rearrange("p o h -> p (o h)").unsqueeze(2).broadcast_to([P, HEADS, HD]),
                                           ALU.mult))
                own.link(dve.tensor_tensor(tmpr[:].rearrange("p (h d) -> p h d", h=HEADS),
                                           g.SBr[:, bass.ds(a, 1), :].rearrange("p o (h d) -> p (o h) d", h=HEADS),
                                           heads_bcast(g.CD[0:HD, NT, 8:16]), ALU.mult))
                dve.wait_ge(states_done, n + 1)
                if not isinstance(n, int):
                    dve.wait_ge(out_stored, 32)
                own.link(dve.tensor_tensor(g.SB[:, bass.ds(b, 1), :].rearrange("p o c -> p (o c)"), tmp[:], g.ps[2][:], ALU.add))
                own.link(dve.tensor_tensor(g.SBr[:, bass.ds(b, 1), :].rearrange("p o c -> p (o c)"), tmpr[:], g.ps[3][0:HD, :], ALU.add))
                dve.sem_inc(state_ready, 1)
            steps(dve, step)

        @block.tensor
        def _(pe):
            def step(n, s, t, a, b):
                pe.wait_ge(loaded[s], (n // 2) * 32 + 32)
                pe.wait_ge(state_ready, n + 2)
                for c in range(6):
                    mm = pe.transpose(g.ps[c // 4][:, (c % 4) * P:(c % 4 + 1) * P], xb[s][:, c, :], g.ident[:])
                mm.then_inc(turned, 1)
                pe.wait_ge(xw_ready, n + 1)
                for gr in range(2):
                    pe.matmul(g.ps[2][:, gr * 256:(gr + 1) * 256], rec[s][:, W_ + gr * P:W_ + (gr + 1) * P],
                              xw[:, gr * 256:(gr + 1) * 256], start=True, stop=True)
                pe.wait_ge(vw_ready, n + 1)
                pe.wait_ge(k_ready, n + 1)
                for h in range(HEADS):
                    k = rec[s][:, W_ + 2 * P + W_ + h * HD:][:, 0:HD]
                    mm = pe.matmul(g.ps[3][0:HD, h * HD:(h + 1) * HD], k, vw[:, h * HD:(h + 1) * HD], start=True, stop=True)
                mm.then_inc(states_done, 1)
            steps(pe, step)


def forward_scan(nc, g):
    with ExitStack() as ctx:
        sb = lambda n, s, d=F32: ctx.enter_context(nc.sbuf_tensor(n, s, d))
        sems = []
        sem = lambda n: new_sem(nc, ctx, f"fw_{n}", sems)
        zvg = [sb(f"zvg{i}", [P, 3 * W_]) for i in range(2)]
        bc = [sb(f"bc{i}", [P, 4, P]) for i in range(2)]
        rec = [sb(f"fwrec{i}", [P, REC]) for i in range(2)]
        qkT = sb("qkT", [HD, 16, P])
        dec = sb("dec", [P, 16, P])
        M, Mr = dec[:, 0:8, :], sb("Mr", [P, HEADS, P])
        xt = [sb(f"fwx{i}", [P, D]) for i in range(2)]
        sf, sfr = sb("sf", [P, W_]), sb("sfr", [HD, W_])
        xw, vw, xd = sb("fwxw", [P, W_]), sb("fwvw", [P, W_]), sb("xd", [P, W_])
        y, t1, t2 = sb("y", [P, W_]), sb("t1", [P, W_]), sb("t2", [P, W_])
        r, r2 = sb("r", [P, W_]), sb("r2", [P, W_])
        gate = sb("gate", [P, 2, W_])
        ycat, yT = sb("ycat", [P, 2 * W_]), sb("yT", [P, KD, P])
        st = sb("fwst", [P, 9])
        mean = sb("mean", [P, HEADS])
        skip, nw, gw, gb = (sb(f"fw{n}", [P, W_]) for n in ("skip", "nw", "gw", "gb"))
        g1 = sb("g1", [P, 2, D])
        wo = g.hT[:, :, 0:D]
        small, loaded, x_stored = sem("small"), [sem("ld0"), sem("ld1")], [sem("xs0"), sem("xs1")]
        (qkT_done, qkT_ready, st_done, seg_done, dec_ready, d1_ready, M_ready, sr_done, Mr_ready, ssd_done, ret_done,
         weighed, xd_ready, y_read, r_read, new_states, state_ready, gates_ready, ms_ready, root_done, ycat_ready,
         yT_done, yT_ready, out_done, mixed, out_stored, chain, zeroed) = (
            sem(n) for n in ("qkTd", "qkTr", "std", "seg", "dec", "d1", "M", "sr", "Mr", "ssd", "ret",
                             "weighed", "xd", "yread", "rread", "news", "state", "gates", "ms", "root", "ycat",
                             "yTd", "yTr", "outd", "mixed", "outst", "chain", "zeroed"))
        h8 = lambda ap: ap.rearrange("p (h d) -> p h d", h=HEADS)
        row8 = lambda tt, t, d: tt[:, bass.ds(t, 1), 8 * d:8 * d + 8].rearrange("p o h -> p (o h)")
        ctx.callback(clear_sems, nc, sems)
        block = ctx.enter_context(nc.Block())

        def steps(eng, body):
            body(0, 0, 0, 0)
            with eng.Fori(0, (NT - 1) // 2) as i:
                body(i * 2 + 1, 1, 1, i * 2 + 2)
                body(i * 2 + 2, 0, 1, i * 2 + 3)

        @block.sync
        def _(sp):
            for dst, src in ((skip[:], bcast_rows(g.skip_row)), (nw[:], bcast_rows(g.ssm_w)), (gw[:], bcast_rows(g.gn_w)),
                             (gb[:], bcast_rows(g.gn_b)), (g1[:, 0], bcast_rows(g.mod_d[0, 2 * D:3 * D])),
                             (g1[:, 1], bcast_rows(g.mod_d[1, 2 * D:3 * D])), (wo, g.w_out.rearrange("(k p) n -> p k n", p=P))):
                sp.dma_start(dst, src).then_inc(small, 16)
            sp.sem_inc(mixed, 2)
            sp.sem_inc(x_stored[0], 16)
            sp.sem_inc(x_stored[1], 16)

            def load(n, s, seq, b):
                sp.wait_ge(mixed, n + 1)
                sp.wait_ge(x_stored[s], (n // 2) * 16 + 16)
                rows = bass.ds(n * P, P)
                for dst, src in ((zvg[s][:, 0:W_], g.tok_d[rows, 0:W_]), (zvg[s][:, W_:], g.tok_d[rows, 3 * W_:5 * W_]),
                                 (bc[s][:], g.xbc_d[4 * P:, :].rearrange("(c p) t -> p c t", p=P)[:, :, rows]),
                                 (rec[s][:], g.rec_d[rows, :]), (xt[s][:], g.x_all[rows, :])):
                    sp.dma_start(dst, src).then_inc(loaded[s], 16)
                if isinstance(n, int):
                    sp.wait_ge(state_ready, 1)
                    sp.dma_start(g.ssd_f_out, sf[:]).then_inc(out_stored, 16)
                    sp.dma_start(g.ret_f_out, sfr[:]).then_inc(out_stored, 16)
                    sp.wait_ge(out_stored, 32)
                    sp.dma_start(sf[:], g.ssd_fwd_T).then_inc(out_stored, 16)
                    sp.dma_start(sfr[:], g.ret_fwd_T).then_inc(out_stored, 16)
            steps(sp, load)
            for s in range(2):
                sp.wait_ge(x_stored[s], 16 * (NT // 2 + 2 - s))

        @block.gpsimd
        def _(pool):
            pool.wait_ge(small, 7 * 16)

            def step(n, s, seq, b):
                pool.wait_ge(loaded[s], (n // 2) * 80 + 80)
                if not isinstance(n, int):
                    pool.wait_ge(state_ready, n)
                    pool.wait_ge(y_read, n)
                x8 = h8(rec[s][:, 0:W_])
                pool.tensor_tensor(h8(xw[:]), x8, row8(g.WD, n, 0).unsqueeze(2).broadcast_to([P, HEADS, HD]), ALU.mult).then_inc(weighed, 1)
                pool.tensor_tensor(h8(vw[:]), h8(zvg[s][:, W_:2 * W_]), heads_bcast(g.WD[:, NT, 0:8]), ALU.mult).then_inc(weighed, 1)
                pool.tensor_tensor(xd[:], rec[s][:, 0:W_], skip[:], ALU.mult).then_inc(xd_ready, 1)
                pool.wait_ge(dec_ready, n * 4 + 4)
                pool.tensor_tensor(dec[:, 8:16, :], dec[:, 8:16, :],
                                   row8(g.DT, n, 1).unsqueeze(2).broadcast_to([P, HEADS, P]), ALU.mult).then_inc(d1_ready, 1)
            steps(pool, step)

        @block.scalar
        def _(act):
            def step(n, s, seq, b):
                act.wait_ge(loaded[s], (n // 2) * 80 + 80)
                act.wait_ge(qkT_done, n + 1)
                if not isinstance(n, int):
                    act.wait_ge(new_states, n)
                for q in range(4):
                    z = act.activation(qkT[:, 4 * q:4 * q + 4, :].rearrange("p h t -> p (h t)"), g.ps[q][0:HD, :], ACT.Copy)
                    z.then_inc(qkT_ready, 1)
                if not isinstance(n, int):
                    act.wait_ge(M_ready, n)
                for q in range(4):
                    act.wait_ge(seg_done, n * 4 + q + 1)
                    for h in range(4):
                        c = 4 * q + h
                        z = act.activation(dec[:, c, :], g.ps[(5, 6, 7, 0)[q]][:, h * P:(h + 1) * P], ACT.Exp,
                                           bias=g.NC[:, bass.ds(n, 1), c])
                    z.then_inc(dec_ready, 1)
                if not isinstance(n, int):
                    act.wait_ge(ycat_ready, n)
                act.activation(gate[:, 0, :], zvg[s][:, 0:W_], ACT.Silu)
                act.activation(gate[:, 1, :], zvg[s][:, 2 * W_:], ACT.Silu).then_inc(gates_ready, 1)
                act.wait_ge(ms_ready, n + 1)
                act.activation(st[:], st[:], ACT.Sqrt).then_inc(root_done, 1)
                act.wait_ge(yT_done, n + 1)
                if not isinstance(n, int):
                    act.wait_ge(mixed, n + 2)
                for q in range(2):
                    z = act.activation(yT[:, 4 * q:4 * q + 4, :].rearrange("p k t -> p (k t)"), g.ps[(3, 5)[q]][:], ACT.Copy)
                z.then_inc(yT_ready, 1)
                act.wait_ge(mixed, n + 3)
                act.dma_start(g.x1_d[bass.ds(n * P, P), :], xt[s][:]).then_inc(x_stored[s], 16)
            steps(act, step)

        @block.vector
        def _(dve):
            own = Chain(dve, chain)
            own.link(dve.memset(sf[:], 0.0))
            own.link(dve.memset(sfr[:], 0.0))
            dve.sem_inc(zeroed, 1)
            dve.wait_ge(small, 7 * 16)
            PRE = own.n

            def link(ins):
                ins.then_inc(chain, 1)
                own.n += 1
                dve.wait_ge(chain, own.base + own.n + PRE)

            def step(n, s, seq, b):
                own.step(n)
                dve.wait_ge(loaded[s], (n // 2) * 80 + 80)
                dve.wait_ge(dec_ready, n * 4 + 2)
                link(dve.tensor_tensor(dec[:, 0:8, :], dec[:, 0:8, :], row8(g.DT, n, 0).unsqueeze(2).broadcast_to([P, HEADS, P]), ALU.mult))
                dve.wait_ge(d1_ready, n + 1)
                link(dve.tensor_tensor(dec[:, 0:8, :], dec[:, 0:8, :], dec[:, 8:16, :], ALU.add))
                dve.wait_ge(st_done, n + 1)
                for gr in range(2):
                    z = dve.tensor_tensor(M[:, 4 * gr:4 * gr + 4, :], dec[:, 4 * gr:4 * gr + 4, :],
                                          g.ps[4][:, gr * P:(gr + 1) * P].unsqueeze(1).broadcast_to([P, 4, P]), ALU.mult)
                    link(z)
                dve.sem_inc(M_ready, 1)
                dve.wait_ge(sr_done, n + 1)
                for q in range(2):
                    link(dve.tensor_tensor(Mr[:, 4 * q:4 * q + 4, :].rearrange("p h t -> p (h t)"),
                                           g.Dret[:, 4 * q:4 * q + 4, :].rearrange("p h t -> p (h t)"), g.ps[1 + q][:], ALU.mult))
                dve.sem_inc(Mr_ready, 1)
                dve.wait_ge(ssd_done, n + 1)
                dve.tensor_tensor(h8(t1[:]), h8(g.ps[3][:]), row8(g.EC, n, 0).unsqueeze(2).broadcast_to([P, HEADS, HD]), ALU.mult)
                link(dve.tensor_tensor(h8(t2[:]), h8(g.ps[5][:]), row8(g.EC, n, 1).unsqueeze(2).broadcast_to([P, HEADS, HD]), ALU.mult))
                link(dve.tensor_tensor(t1[:], t1[:], g.ps[6][:], ALU.add))
                dve.wait_ge(xd_ready, n + 1)
                link(dve.tensor_tensor(t2[:], t2[:], xd[:], ALU.add))
                dve.sem_inc(y_read, 1)
                link(dve.tensor_tensor(y[:], t1[:], t2[:], ALU.add))
                dve.wait_ge(gates_ready, n + 1)
                link(dve.tensor_tensor(y[:], y[:], gate[:, 0, :], ALU.mult))
                link(dve.tensor_tensor_reduce(t1[:], y[:], y[:], 1.0 / W_, EPS, ALU.mult, ALU.add, st[:, 0:1]))
                dve.wait_ge(ret_done, n + 1)
                dve.tensor_tensor(h8(r[:]), h8(g.ps[7][:]), heads_bcast(g.EC[:, NT, 0:8]), ALU.mult)
                link(dve.tensor_tensor(h8(r2[:]), h8(g.ps[0][:]), heads_bcast(g.EC[:, NT, 8:16]), ALU.mult))
                link(dve.tensor_tensor(r[:], r[:], g.ps[4][:], ALU.add))
                dve.sem_inc(r_read, 1)
                link(dve.tensor_tensor(r[:], r[:], r2[:], ALU.add))
                link(dve.tensor_reduce(mean[:], h8(r[:]), AXX, ALU.add))
                link(dve.tensor_scalar(mean[:], mean[:], 1.0 / HD, None, ALU.mult))
                link(dve.tensor_tensor(h8(r[:]), h8(r[:]), heads_bcast(mean[:]), ALU.subtract))
                link(dve.tensor_tensor(r2[:], r[:], r[:], ALU.mult))
                link(dve.tensor_reduce(st[:, 1:9], h8(r2[:]), AXX, ALU.add))
                link(dve.tensor_scalar(st[:, 1:9], st[:, 1:9], 1.0 / HD, EPS, ALU.mult, ALU.add))
                dve.sem_inc(ms_ready, 1)
                dve.wait_ge(new_states, n + 1)
                if not isinstance(n, int):
                    dve.wait_ge(out_stored, 64)
                dve.tensor_tensor(h8(sf[:]), h8(sf[:]), row8(g.CD, n, 0).unsqueeze(2).broadcast_to([P, HEADS, HD]), ALU.mult)
                link(dve.tensor_tensor(h8(sfr[:]), h8(sfr[:]), heads_bcast(g.CD[0:HD, NT, 0:8]), ALU.mult))
                dve.tensor_tensor(sf[:], sf[:], g.ps[1][:], ALU.add)
                link(dve.tensor_tensor(sfr[:], sfr[:], g.ps[2][0:HD, :], ALU.add))
                dve.sem_inc(state_ready, 1)
                dve.wait_ge(root_done, n + 1)
                link(dve.reciprocal(st[:], st[:]))
                dve.scalar_tensor_tensor(ycat[:, 0:W_], y[:], st[:, 0:1], nw[:], ALU.mult, ALU.mult)
                link(dve.tensor_tensor(h8(r[:]), h8(r[:]), heads_bcast(st[:, 1:9]), ALU.mult))
                link(dve.tensor_tensor(r[:], r[:], gw[:], ALU.mult))
                link(dve.tensor_tensor(r[:], r[:], gb[:], ALU.add))
                link(dve.tensor_tensor(ycat[:, W_:], r[:], gate[:, 1, :], ALU.mult))
                dve.sem_inc(ycat_ready, 1)
                dve.wait_ge(out_done, n + 1)
                dve.tensor_tensor(t1[:], g.ps[6][:], g1[:, seq, 0:512], ALU.mult)
                link(dve.tensor_tensor(t2[:], g.ps[7][:], g1[:, seq, 512:], ALU.mult))
                for q, tt in enumerate((t1, t2)):
                    x = xt[s][:, q * 512:(q + 1) * 512]
                    z = dve.tensor_tensor(x, x, tt[:], ALU.add)
                    if q == 0:
                        z.then_inc(chain, 1)
                        own.n += 1
                    else:
                        link(z)
                dve.sem_inc(mixed, 1)
            steps(dve, step)

        @block.tensor
        def _(pe):
            pe.wait_ge(small, 7 * 16)

            def step(n, s, seq, b):
                first = isinstance(n, int)
                pe.wait_ge(loaded[s], (n // 2) * 80 + 80)
                if not first:
                    pe.wait_ge(state_ready, n)
                    pe.wait_ge(yT_ready, n)
                qk = W_ + 2 * P
                for gr in range(2):
                    mm = pe.matmul(g.ps[4][:, gr * P:(gr + 1) * P], bc[s][:, gr, :], bc[s][:, 2 + gr, :], start=True, stop=True)
                mm.then_inc(st_done, 1)
                for c in range(16):
                    mm = pe.transpose(g.ps[c // 4][0:HD, (c % 4) * P:(c % 4 + 1) * P], rec[s][:, qk + c * HD:qk + (c + 1) * HD], g.ident[:])
                mm.then_inc(qkT_done, 1)
                for q in range(4):
                    if q == 1 and not first:
                        pe.wait_ge(mixed, n + 2)
                    if q == 3:
                        pe.wait_ge(qkT_ready, n * 4 + 4)
                    segment(pe, g, q, g.ps[(5, 6, 7, 0)[q]], n).then_inc(seg_done, 1)
                for h in range(HEADS):
                    mm = pe.matmul(g.ps[1 + h // 4][:, (h % 4) * P:(h % 4 + 1) * P], qkT[:, 8 + h, :], qkT[:, h, :], start=True, stop=True)
                mm.then_inc(sr_done, 1)
                pe.wait_ge(dec_ready, n * 4 + 1)
                if not first:
                    pe.wait_ge(out_stored, 64)
                pe.wait_ge(zeroed, 1)
                for gr in range(2):
                    c = bc[s][:, 2 + gr, :]
                    cols = slice(gr * 256, (gr + 1) * 256)
                    pe.matmul(g.ps[3][:, cols], c, sf[:, cols], start=True, stop=True)
                    pe.matmul(g.ps[5][:, cols], c, g.SB[:, bass.ds(b, 1), cols].rearrange("p o c -> p (o c)"), start=True, stop=True)
                pe.wait_ge(M_ready, n + 1)
                for h in range(HEADS):
                    cols = slice(h * HD, (h + 1) * HD)
                    mm = pe.matmul(g.ps[6][:, cols], M[:, h, :], rec[s][:, cols], start=True, stop=True)
                mm.then_inc(ssd_done, 1)
                for h in range(HEADS):
                    cols = slice(h * HD, (h + 1) * HD)
                    pe.matmul(g.ps[7][:, cols], qkT[:, h, :], sfr[:, cols], start=True, stop=True)
                    pe.matmul(g.ps[0][:, cols], qkT[:, h, :], g.SBr[:, bass.ds(b, 1), cols].rearrange("p o c -> p (o c)"), start=True, stop=True)
                pe.wait_ge(Mr_ready, n + 1)
                for h in range(HEADS):
                    cols = slice(h * HD, (h + 1) * HD)
                    mm = pe.matmul(g.ps[4][:, cols], Mr[:, h, :], zvg[s][:, W_ + h * HD:W_ + (h + 1) * HD], start=True, stop=True)
                mm.then_inc(ret_done, 1)
                pe.wait_ge(weighed, n * 2 + 2)
                for gr in range(2):
                    cols = slice(gr * 256, (gr + 1) * 256)
                    pe.matmul(g.ps[1][:, cols], rec[s][:, W_ + gr * P:W_ + (gr + 1) * P], xw[:, cols], start=True, stop=True)
                for h in range(HEADS):
                    cols = slice(h * HD, (h + 1) * HD)
                    k = rec[s][:, qk + W_ + h * HD:qk + W_ + (h + 1) * HD]
                    mm = pe.matmul(g.ps[2][0:HD, cols], k, vw[:, cols], start=True, stop=True)
                mm.then_inc(new_states, 1)
                pe.wait_ge(ycat_ready, n + 1)
                for k in range(KD):
                    mm = pe.transpose(g.ps[(3, 5)[k // 4]][:, (k % 4) * P:(k % 4 + 1) * P], ycat[:, k * P:(k + 1) * P], g.ident[:])
                mm.then_inc(yT_done, 1)
                pe.wait_ge(yT_ready, n + 1)
                for q in range(2):
                    for k in range(KD):
                        mm = pe.matmul(g.ps[6 + q][:], yT[:, k, :], wo[:, k, q * 512:(q + 1) * 512], start=(k == 0), stop=(k == KD - 1))
                mm.then_inc(out_done, 1)
            steps(pe, step)


def expert_scores(nc, g):
    TG, NH = 384, 2 * HEADS
    with ExitStack() as ctx:
        sb = lambda n, s, d=F32: ctx.enter_context(nc.sbuf_tensor(n, s, d))
        sems = []
        sem = lambda n: new_sem(nc, ctx, f"es_{n}", sems)
        wq = [sb(f"wq{i}", [P, KD, P]) for i in range(2)]
        qT = [sb(f"qT{i}", [P, T]) for i in range(2)]
        keys = sb("keys", [P, NH, NKEY])
        small, w_loaded, hT_stored = sem("small"), [sem("w0"), sem("w1")], sem("hst")
        q_done, qT_ready, s_done, s_copied = sem("q"), sem("qT"), sem("s"), sem("sc")
        wv = g.peer_wq.rearrange("(k p) n -> p k n", p=P)
        PARTS = ((0, 4), (4, 8), (8, 9))
        bank_of = lambda s, j: 6 + (s + j) % 2
        ctx.callback(clear_sems, nc, sems)
        block = ctx.enter_context(nc.Block())

        @block.sync
        def _(sp):
            sp.dma_start(keys[:], g.keys_T).then_inc(small, 16)
            for s in range(2):
                sp.dma_start(wq[s][:], wv[:, :, s * P:(s + 1) * P]).then_inc(w_loaded[s], 16)
            sp.dma_start(g.h2T_d, g.hT[:]).then_inc(hT_stored, 16)
            with sp.Fori(0, NH // 2 - 1) as i:
                for s in range(2):
                    sp.wait_ge(q_done, i * 2 + s + 1)
                    sp.dma_start(wq[s][:], wv[:, :, bass.ds(i * (2 * P) + (2 + s) * P, P)]).then_inc(w_loaded[s], 16)
            sp.wait_ge(hT_stored, 16)

        @block.tensor
        def _(pe):
            def query(n, s, i):
                pe.wait_ge(w_loaded[s], i * 16 + 16)
                for b in range(T // TG):
                    for k in range(KD):
                        mm = pe.matmul(g.ps[3 * s + b][:, 0:TG], wq[s][:, k, :], g.hT[:, k, b * TG:(b + 1) * TG],
                                       start=(k == 0), stop=(k == KD - 1))
                mm.then_inc(q_done, 1)

            def score(n, s):
                pe.wait_ge(qT_ready, n + 1)
                for j, (a, b) in enumerate(PARTS):
                    bank = bank_of(s, j)
                    pe.wait_ge(s_copied, n * 3 + j + 1)
                    for t in range(a, b):
                        mm = pe.matmul(g.ps[bank][:, (t - a) * P:(t - a + 1) * P], qT[s][:, t * P:(t + 1) * P],
                                       keys[:, bass.ds(n, 1), :].rearrange("p o c -> p (o c)"), start=True, stop=True)
                    mm.then_inc(s_done, 1)
            pe.wait_ge(small, 16)
            query(0, 0, 0)
            query(1, 1, 0)
            with pe.Fori(0, NH // 2 - 1) as i:
                for s in range(2):
                    score(i * 2 + s, s)
                    query(i * 2 + s + 2, s, i + 1)
            score(NH - 2, 0)
            score(NH - 1, 1)

        @block.scalar
        def _(act):
            with act.Fori(0, NH // 2) as i:
                for s in range(2):
                    n = i * 2 + s
                    act.wait_ge(q_done, n + 1)
                    for b in range(T // TG):
                        z = act.activation(qT[s][:, b * TG:(b + 1) * TG], g.ps[3 * s + b][:, 0:TG], ACT.Copy)
                    z.then_inc(qT_ready, 1)

        @block.vector
        def _(dve):
            dve.sem_inc(s_copied, 2)
            with dve.Fori(0, NH // 2) as i:
                for s in range(2):
                    n = i * 2 + s
                    for j, (a, b) in enumerate(PARTS):
                        dve.wait_ge(s_done, n * 3 + j + 1)
                        dve.tensor_copy(g.SC[:, a:b, bass.ds(n, 1), :].rearrange("p t o c -> p t (o c)"),
                                        g.ps[bank_of(s, j)][:, 0:(b - a) * P].rearrange("p (t c) -> p t c", c=P)).then_inc(s_copied, 1)


def select_experts(nc, g):
    NH = 2 * HEADS
    with ExitStack() as ctx:
        sb = lambda n, s, d=F32: ctx.enter_context(nc.sbuf_tensor(n, s, d))
        sems = []
        sem = lambda n: new_sem(nc, ctx, f"tk_{n}", sems)
        sc = [sb(f"tksc{i}", [P, NH, NKEY]) for i in range(2)]
        best, place = sb("best", [P, NH, TOPK]), sb("place", [P, NH, TOPK], U32)
        placef = sb("placef", [P, HEADS, 2, TOPK])
        cand = sb("cand", [P, HEADS, TOPK, TOPK])
        top, pos = sb("top", [P, HEADS, TOPK]), sb("pos", [P, HEADS, TOPK], U32)
        ab, abf = sb("ab", [P, 2, NSEL], U32), sb("abf", [P, 2, NSEL])
        hit = [sb(f"hit{i}", [P, NSEL, TOPK]) for i in range(2)]
        out3 = sb("out3", [P, 3, NSEL])
        den = sb("den", [P, HEADS])
        iota16 = sb("iota16", [P, TOPK])
        small, copied, top_ready, exp_ready, ab_ready, hit_ready, out_ready, turned, done, chain, pchain = (
            sem(n) for n in ("small", "copied", "top", "exp", "ab", "hit", "out", "turned", "done", "chain", "pchain"))
        pad, ppad = sb("tkpad", [P, 1]), sb("tkppad", [P, 1])
        i16 = iota16[:].unsqueeze(1).broadcast_to([P, NSEL, TOPK])
        ctx.callback(clear_sems, nc, sems)
        block = ctx.enter_context(nc.Block())

        def tiles(eng, body):
            body(0, 0)
            with eng.Fori(0, (NT - 1) // 2) as i:
                body(i * 2 + 1, 1)
                body(i * 2 + 2, 0)

        def spread(p):
            return placef[:, :, p, :].unsqueeze(2).broadcast_to([P, HEADS, TOPK, TOPK])

        @block.sync
        def _(sp):
            sp.dma_start(iota16[:], g.iota_d[:, 0:TOPK]).then_inc(small, 16)

        @block.scalar
        def _(act):
            act.sem_inc(done, 1)

            def copy(n, s):
                if not isinstance(n, int):
                    act.wait_ge(top_ready, n)
                act.activation(sc[s][:], g.SC[:, bass.ds(n, 1)].rearrange("p o h c -> p (o h) c"), ACT.Copy).then_inc(copied, 1)

            def tile(n, s):
                copy(n, s)
                act.wait_ge(top_ready, n + 1)
                act.activation(out3[:, 2], out3[:, 2], ACT.Exp).then_inc(exp_ready, 1)
                act.wait_ge(turned, n + 1)
                act.activation(g.sel3[:, :, bass.ds(n * P, P)], g.ps[0][:, 0:3 * P].rearrange("p (c t) -> p c t", c=3), ACT.Copy).then_inc(done, 1)
            tiles(act, tile)

        @block.gpsimd
        def _(pool):
            pool.wait_ge(small, 16)

            def tile(n, s):
                pool.wait_ge(ab_ready, n + 1)
                if not isinstance(n, int):
                    pool.wait_ge(out_ready, n)
                pool.tensor_tensor(hit[0][:], abf[:, 0].unsqueeze(2).broadcast_to([P, NSEL, TOPK]), i16, ALU.subtract).then_inc(pchain, 1)
                pool.wait_ge(pchain, n * 3 + 1)
                pool.tensor_tensor(ppad[:], iota16[:, 0:1], iota16[:, 0:1], ALU.add)
                pool.tensor_scalar(hit[0][:], hit[0][:], 0.0, None, ALU.is_equal).then_inc(pchain, 1)
                pool.wait_ge(pchain, n * 3 + 2)
                h4 = hit[0][:].rearrange("p (h k) a -> p h k a", h=HEADS)
                pool.tensor_tensor(h4, h4, spread(0), ALU.mult).then_inc(pchain, 1)
                pool.wait_ge(pchain, n * 3 + 3)
                pool.sem_inc(hit_ready, 1)
            tiles(pool, tile)

        @block.vector
        def _(dve):
            own = Chain(dve, chain)
            link = own.link
            dve.wait_ge(small, 16)

            def tile(n, s):
                own.step(n)
                dve.wait_ge(copied, n + 1)
                def rounds(values, best_of, place_of, lists):
                    for r in range(2):
                        dve.memset(pad[:], 0.0)
                        for i in range(lists):
                            z = dve.max(best_of(i)[:, 8 * r:8 * r + 8], values(i))
                        link(z)
                        dve.memset(pad[:], 0.0)
                        for i in range(lists):
                            z = dve.max_index(place_of(i)[:, 8 * r:8 * r + 8], best_of(i)[:, 8 * r:8 * r + 8], values(i))
                        link(z)
                        if r == 0:
                            dve.memset(pad[:], 0.0)
                            for i in range(lists):
                                z = dve.match_replace(values(i), best_of(i)[:, 0:8], values(i), LOW)
                            link(z)
                rounds(lambda i: sc[s][:, i, :], lambda i: best[:, i, :], lambda i: place[:, i, :], NH)
                dve.tensor_copy(placef[:].rearrange("p h s k -> p (h s) k"), place[:])
                b4 = best[:].rearrange("p (h s) k -> p h s k", s=2)
                link(dve.tensor_tensor(cand[:], b4[:, :, 0, :].unsqueeze(3).broadcast_to([P, HEADS, TOPK, TOPK]),
                                       b4[:, :, 1, :].unsqueeze(2).broadcast_to([P, HEADS, TOPK, TOPK]), ALU.add))
                rounds(lambda i: cand[:, i].rearrange("p a b -> p (a b)"), lambda i: top[:, i, :], lambda i: pos[:, i, :], HEADS)
                if not isinstance(n, int):
                    dve.wait_ge(turned, n)
                o = out3[:, 2].rearrange("p (h k) -> p h k", h=HEADS)
                link(dve.tensor_tensor(o, top[:], top[:, :, 0:1].broadcast_to([P, HEADS, TOPK]), ALU.subtract))
                dve.sem_inc(top_ready, 1)
                p1 = pos[:].rearrange("p h k -> p (h k)")
                dve.tensor_scalar(ab[:, 0], p1, 4, None, ALU.logical_shift_right)
                link(dve.tensor_scalar(ab[:, 1], p1, 15, None, ALU.bitwise_and))
                link(dve.tensor_copy(abf[:], ab[:]))
                dve.sem_inc(ab_ready, 1)
                link(dve.tensor_tensor(hit[1][:], abf[:, 1].unsqueeze(2).broadcast_to([P, NSEL, TOPK]), i16, ALU.is_equal))
                h4 = hit[1][:].rearrange("p (h k) a -> p h k a", h=HEADS)
                link(dve.tensor_tensor(h4, h4, spread(1), ALU.mult))
                link(dve.tensor_reduce(out3[:, 1], hit[1][:], AXX, ALU.add))
                dve.wait_ge(exp_ready, n + 1)
                link(dve.tensor_reduce(den[:], o, AXX, ALU.add))
                link(dve.reciprocal(den[:], den[:]))
                link(dve.tensor_tensor(o, o, den[:].unsqueeze(2).broadcast_to([P, HEADS, TOPK]), ALU.mult))
                dve.wait_ge(hit_ready, n + 1)
                link(dve.tensor_reduce(out3[:, 0], hit[0][:], AXX, ALU.add))
                dve.sem_inc(out_ready, 1)
            tiles(dve, tile)

        @block.tensor
        def _(pe):
            def tile(n, s):
                pe.wait_ge(out_ready, n + 1)
                pe.wait_ge(done, n + 1)
                for c in range(3):
                    mm = pe.transpose(g.ps[0][:, c * P:(c + 1) * P], out3[:, c], g.ident[:])
                mm.then_inc(turned, 1)
            tiles(pe, tile)


def dense_gates(nc, g):
    G, B = 8, 2
    RT = P // G
    with ExitStack() as ctx:
        sb = lambda n, s, d=F32: ctx.enter_context(nc.sbuf_tensor(n, s, d))
        sems = []
        sem = lambda n: new_sem(nc, ctx, f"dg_{n}", sems)
        one, two = sb("one_hot1", [P, 2 * G, P]), sb("one_hot2", [P, 2 * G, P])
        iota = sb("iota", [P, P])
        out = [sb(f"gates{i}", [P, NKEY, P]) for i in range(2)]
        small, one_ready, prod, copied, stored = (sem(n) for n in ("small", "one", "prod", "copied", "stored"))
        stored = [stored, sem("stored1")]
        ctx.callback(clear_sems, nc, sems)
        block = ctx.enter_context(nc.Block())

        def tiles(eng, body):
            body(0, 0)
            with eng.Fori(0, (NT - 1) // 2) as i:
                body(i * 2 + 1, 1)
                body(i * 2 + 2, 0)

        def hot(eng, ready, makes):
            eng.wait_ge(small, 16)
            with eng.Fori(0, T // (2 * G)) as i:
                for s in range(2):
                    r = i * 2 + s
                    eng.wait_ge(prod, r * B + B)
                    for j in range(G):
                        for make in makes:
                            z = make(s * G + j, i * (2 * G) + (s * G + j))
                    z.then_inc(ready, 1)

        @block.sync
        def _(sp):
            sp.dma_start(iota[:], g.iota_d).then_inc(small, 16)
            sp.sem_inc(stored[0], 16)
            sp.sem_inc(stored[1], 16)
            sp.sem_inc(prod, 2 * B)

            def store(t, s):
                sp.wait_ge(copied, t * (RT * B) + (RT * B + 2 * B))
                sp.dma_start(g.gates_d.rearrange("b a t -> a b t")[:, :, bass.ds(t * P, P)], out[s][:]).then_inc(stored[s], 16)
            tiles(sp, store)
            sp.wait_ge(stored[0], 16 * 6)
            sp.wait_ge(stored[1], 16 * 5)

        @block.vector
        def _(dve):
            hot(dve, one_ready, (lambda j, t: dve.tensor_scalar(one[:, j], iota[:], g.sel3[:, 0, bass.ds(t, 1)],
                                                                g.sel3[:, 2, bass.ds(t, 1)], ALU.is_equal, ALU.mult),
                                 lambda j, t: dve.tensor_scalar(two[:, j], iota[:], g.sel3[:, 1, bass.ds(t, 1)], None, ALU.is_equal)))

        @block.tensor
        def _(pe):
            with pe.Fori(0, T // (2 * G)) as i:
                for s in range(2):
                    r = i * 2 + s
                    pe.wait_ge(one_ready, r + 1)
                    for b in range(B):
                        pe.wait_ge(copied, r * B + b + 1)
                        for j in range(G // B):
                            q = s * G + b * (G // B) + j
                            mm = pe.matmul(g.ps[2 * s + b][:, j * P:(j + 1) * P], one[:, q], two[:, q], start=True, stop=True)
                        mm.then_inc(prod, 1)

        @block.scalar
        def _(act):
            act.sem_inc(copied, 2 * B)

            def tile(t, s):
                act.wait_ge(stored[s], (t // 2) * 16 + 16)
                with act.Fori(0, RT // 2) as i:
                    for h in range(2):
                        for b in range(B):
                            act.wait_ge(prod, t * (RT * B) + i * (2 * B) + (h * B + b + 1 + 2 * B))
                            first = i * (2 * G) + (h * G + b * (G // B))
                            act.activation(out[s][:, :, bass.ds(first, G // B)].rearrange("p c t -> p t c"),
                                           g.ps[2 * h + b][:].rearrange("p (t c) -> p t c", c=P), ACT.Copy).then_inc(copied, 1)
            tiles(act, tile)


def experts(nc, g):
    TG, NE = 384, NKEY
    NB = T // TG
    with ExitStack() as ctx:
        sb = lambda n, s, d=F32: ctx.enter_context(nc.sbuf_tensor(n, s, d))
        sems = []
        sem = lambda n: new_sem(nc, ctx, f"ex_{n}", sems)
        pair = lambda n, s, d=F32: [sb(f"{n}{i}", s, d) for i in range(2)]
        h_hi, h_lo = sb("h_hi", [P, KD, T], F32R), sb("h_lo", [P, KD, T], F32R)
        uw, u_hi, u_lo = pair("uw", [P, KD, P]), pair("u_hi", [P, KD, P], F32R), pair("u_lo", [P, KD, P], F32R)
        vw, v_hi, v_lo = pair("vw", [P, D]), pair("v_hi", [P, D], F32R), pair("v_lo", [P, D], F32R)
        gt, a, a_hi, a_lo = pair("gt", [P, T]), pair("ga", [P, T]), pair("a_hi", [P, T], F32R), pair("a_lo", [P, T], F32R)
        f = lambda ap: ap.bitcast(F32)
        psem = lambda n: [sem(n + "0"), sem(n + "1")]
        h_loaded, u_loaded, v_loaded, g_loaded = psem("h"), psem("ul"), psem("vl"), psem("gl")
        (h_hi_ready, h_lo_ready, u_hi_ready, u_lo_ready, v_hi_ready, v_lo_ready, s_done, act_done, a_ready, a_hi_ready,
         a_lo_ready, y_done, y_added, zeroed) = (
            sem(n) for n in ("hhi", "hlo", "uhi", "ulo", "vhi", "vlo", "s", "act", "a", "ahi", "alo", "y", "yadd", "z"))
        ctx.callback(clear_sems, nc, sems)
        block = ctx.enter_context(nc.Block())
        YP = 2 * NT

        def load_u(sp, e, s):
            sp.dma_start(uw[s][:], g.u_T[bass.ds(e, 1)].rearrange("o p k c -> p (o k) c")).then_inc(u_loaded[s], 16)

        def load_v(sp, e, s):
            sp.dma_start(vw[s][:], g.peer_v[:, bass.ds(e, 1), :].rearrange("p o d -> p (o d)")).then_inc(v_loaded[s], 16)

        def load_g(sp, e, s):
            sp.dma_start(gt[s][:], g.gates_d[bass.ds(e, 1)].rearrange("o p t -> p (o t)")).then_inc(g_loaded[s], 16)

        @block.sync
        def _(sp):
            for k in range(KD):
                s = k % 2
                if k >= 2:
                    sp.wait_ge(h_lo_ready, k - 1)
                sp.dma_start(gt[s][:], g.h2T_d[:, k, :]).then_inc(h_loaded[s], 16)
                if k < 2:
                    load_u(sp, k, k)
                    load_v(sp, k, k)
            for s in range(2):
                sp.wait_ge(h_lo_ready, KD - 1 + s)
                load_g(sp, s, s)
            with sp.Fori(1, NE // 2) as j:
                for s in range(2):
                    e = j * 2 + s
                    sp.wait_ge(u_lo_ready, e - 1)
                    sp.wait_ge(u_hi_ready, e - 1)
                    load_u(sp, e, s)
                    sp.wait_ge(a_ready, e - 1)
                    load_g(sp, e, s)
                    sp.wait_ge(v_lo_ready, e - 1)
                    sp.wait_ge(v_hi_ready, e - 1)
                    load_v(sp, e, s)

        def split_u(act, e, s, j):
            act.wait_ge(u_loaded[s], j * 16 + 16)
            act.activation(u_hi[s][:], uw[s][:], ACT.Copy).then_inc(u_hi_ready, 1)

        @block.scalar
        def _(act):
            for k in range(KD):
                s = k % 2
                act.wait_ge(h_loaded[s], 16 * (k // 2 + 1))
                act.activation(h_hi[:, k, :], gt[s][:], ACT.Copy).then_inc(h_hi_ready, 1)
            split_u(act, 0, 0, 0)
            split_u(act, 1, 1, 0)

            def block_(j, s, last=False):
                e = j * 2 + s
                act.wait_ge(s_done, e + 1)
                if not isinstance(j, int):
                    act.wait_ge(a_lo_ready, e - 1)
                for b in range(NB):
                    z = act.activation(a[s][:, b * TG:(b + 1) * TG], g.ps[3 * s + b][:, 0:TG], ACT.Gelu_apprx_tanh)
                z.then_inc(act_done, 1)
                if not last:
                    split_u(act, e + 2, s, j + 1)
                if not isinstance(j, int) or j > 0:
                    if s == 0:
                        act.wait_ge(y_done, j * YP)
                act.wait_ge(v_loaded[s], j * 16 + 16)
                act.activation(v_hi[s][:], vw[s][:], ACT.Copy).then_inc(v_hi_ready, 1)
                act.wait_ge(a_ready, e + 1)
                act.activation(a_hi[s][:], a[s][:], ACT.Copy).then_inc(a_hi_ready, 1)
            block_(0, 0)
            block_(0, 1)
            with act.Fori(1, NE // 2 - 1) as j:
                block_(j, 0)
                block_(j, 1)
            block_(NE // 2 - 1, 0, True)
            block_(NE // 2 - 1, 1, True)

        @block.gpsimd
        def _(pool):
            def low_u(s, e, j):
                pool.wait_ge(u_hi_ready, e + 1)
                pool.tensor_tensor(u_lo[s][:], uw[s][:], f(u_hi[s][:]), ALU.subtract).then_inc(u_lo_ready, 1)
            low_u(0, 0, 0)
            low_u(1, 1, 0)

            def low(j, s, last=False):
                e = j * 2 + s
                if not last:
                    low_u(s, e + 2, j + 1)
                pool.wait_ge(v_hi_ready, e + 1)
                pool.tensor_tensor(v_lo[s][:], vw[s][:], f(v_hi[s][:]), ALU.subtract).then_inc(v_lo_ready, 1)
            with pool.Fori(0, NE // 2 - 1) as j:
                low(j, 0)
                low(j, 1)
            low(NE // 2 - 1, 0, True)
            low(NE // 2 - 1, 1, True)

        @block.vector
        def _(dve):
            dve.memset(g.Y[:], 0.0).then_inc(zeroed, 1)
            for k in range(KD):
                dve.wait_ge(h_hi_ready, k + 1)
                dve.tensor_tensor(h_lo[:, k, :], gt[k % 2][:], f(h_hi[:, k, :]), ALU.subtract).then_inc(h_lo_ready, 1)
            dve.sem_inc(y_added, 2)
            dve.wait_ge(zeroed, 1)

            def gate(j, s):
                e = j * 2 + s
                dve.wait_ge(act_done, e + 1)
                dve.wait_ge(g_loaded[s], j * 16 + 16)
                dve.tensor_tensor(a[s][:], a[s][:], gt[s][:], ALU.mult).then_inc(a_ready, 1)

            def low(j, s):
                dve.wait_ge(a_hi_ready, j * 2 + s + 1)
                dve.tensor_tensor(a_lo[s][:], a[s][:], f(a_hi[s][:]), ALU.subtract).then_inc(a_lo_ready, 1)

            def add(j):
                for m in range(YP):
                    dve.wait_ge(y_done, j * YP + m + 1)
                    y = g.Y[:, m // 2, (m % 2) * 512:(m % 2 + 1) * 512]
                    dve.tensor_tensor(y, y, g.ps[6 + m % 2][:], ALU.add).then_inc(y_added, 1)
            for s in range(2):
                gate(0, s)
                low(0, s)
            with dve.Fori(1, NE // 2) as j:
                gate(j, 0)
                dve.wait_ge(y_added, j * YP - YP + 2)
                add(j - 1)
                low(j, 0)
                gate(j, 1)
                low(j, 1)
            dve.wait_ge(y_added, (NE // 2 - 1) * YP + 2)
            add(NE // 2 - 1)

        @block.tensor
        def _(pe):
            def hidden(j, s):
                e = j * 2 + s
                pe.wait_ge(u_hi_ready, e + 1)
                pe.wait_ge(u_lo_ready, e + 1)
                if not isinstance(j, int):
                    pe.wait_ge(act_done, e - 1)
                for b in range(NB):
                    cols = slice(b * TG, (b + 1) * TG)
                    for k in range(KD):
                        for i, (u, h) in enumerate(((u_hi, h_hi), (u_hi, h_lo), (u_lo, h_hi))):
                            mm = pe.matmul(g.ps[3 * s + b][:, 0:TG], u[s][:, k, :], h[:, k, cols],
                                           start=(k == 0 and i == 0), stop=(k == KD - 1 and i == 2))
                mm.then_inc(s_done, 1)

            def output(j):
                pe.wait_ge(a_lo_ready, j * 2 + 2)
                pe.wait_ge(v_lo_ready, j * 2 + 2)
                for m in range(YP):
                    pe.wait_ge(y_added, j * YP + m + 1)
                    rows, cols = slice((m // 2) * P, (m // 2 + 1) * P), slice((m % 2) * 512, (m % 2 + 1) * 512)
                    for s in range(2):
                        for i, (x, v) in enumerate(((a_hi, v_hi), (a_hi, v_lo), (a_lo, v_hi))):
                            mm = pe.matmul(g.ps[6 + m % 2][:], x[s][:, rows], v[s][:, cols],
                                           start=(s == 0 and i == 0), stop=(s == 1 and i == 2))
                    mm.then_inc(y_done, 1)
            pe.wait_ge(h_lo_ready, KD)
            hidden(0, 0)
            hidden(0, 1)
            with pe.Fori(1, NE // 2) as j:
                hidden(j, 0)
                output(j - 1)
                hidden(j, 1)
            output(NE // 2 - 1)


def final_norm(nc, g):
    with ExitStack() as ctx:
        sb = lambda n, s, d=F32: ctx.enter_context(nc.sbuf_tensor(n, s, d))
        sems = []
        sem = lambda n: new_sem(nc, ctx, f"fn_{n}", sems)
        x = sb("fnx", [P, NT, D])
        g2, lnf, junk = sb("g2", [P, 2, D]), sb("lnfw", [P, D]), sb("fnjunk", [P, D])
        ss = sb("fnss", [P, NT])
        small, loaded, chain, ms_ready, root_done, stored = (sem(n) for n in ("small", "ld", "chain", "ms", "root", "st"))
        ctx.callback(clear_sems, nc, sems)
        block = ctx.enter_context(nc.Block())

        @block.sync
        def _(sp):
            for dst, src in ((g2[:, 0], bcast_rows(g.mod_d[0, 5 * D:6 * D])), (g2[:, 1], bcast_rows(g.mod_d[1, 5 * D:6 * D])),
                             (lnf[:], bcast_rows(g.lnf)), (x[:], g.x1_d.rearrange("(t p) d -> p t d", p=P))):
                sp.dma_start(dst, src).then_inc(small, 16)
            with sp.Fori(0, NT) as t:
                sp.wait_ge(chain, t + (3 * NT + 2))
                sp.dma_start(g.y_all[bass.ds(t * P, P), :], x[:, bass.ds(t, 1), :].rearrange("p o d -> p (o d)")).then_inc(stored, 16)
            sp.wait_ge(stored, 16 * NT)

        @block.scalar
        def _(act):
            act.wait_ge(ms_ready, 1)
            act.activation(ss[:], ss[:], ACT.Sqrt).then_inc(root_done, 1)

        @block.vector
        def _(dve):
            own = Chain(dve, chain)
            dve.wait_ge(small, 64)
            for t in range(NT):
                seq = min(t, 1)
                own.link(dve.tensor_tensor(junk[:], g.Y[:, t], g2[:, seq], ALU.mult))
                own.link(dve.tensor_tensor(x[:, t], x[:, t], junk[:], ALU.add))
                own.link(dve.tensor_tensor_reduce(junk[:], x[:, t], x[:, t], 1.0 / D, EPS, ALU.mult, ALU.add, ss[:, t:t + 1]))
            dve.sem_inc(ms_ready, 1)
            dve.wait_ge(root_done, 1)
            own.link(dve.reciprocal(ss[:], ss[:]))
            for t in range(NT):
                own.link(dve.scalar_tensor_tensor(x[:, t], x[:, t], ss[:, t:t + 1], lnf[:], ALU.mult, ALU.mult))


def program(nc, g, ctx):
    sb = lambda n, s, d=F32: ctx.enter_context(nc.sbuf_tensor(n, s, d))
    g.ps = [ctx.enter_context(nc.psum_tensor(f"ps{i}", [P, 512], F32)) for i in range(8)]
    g.ident = sb("ident", [P, P])
    g.gain, g.shift = sb("gain", [P, 2, KD, 2]), sb("shift", [P, 2, KD, 2])
    with nc.sbuf_tensor("hT", [P, KD, T], F32) as g.hT:
        with nc.sbuf_tensor("X0", [P, NT, D], F32) as g.X:
            modulation(nc, g)
            norm_transpose(nc, g, 0)
        project_in(nc, g)
        with ExitStack() as mixer:
            sb = lambda n, s, d=F32: mixer.enter_context(nc.sbuf_tensor(n, s, d))
            g.DT, g.EC, g.WD, g.CD, g.NC = (sb(n, [P, NR, 16]) for n in ("DT", "EC", "WD", "CD", "NC"))
            g.sel, g.mneg = sb("sel", [16, 16, P]), sb("mneg", [P, 2, 4 * P])
            g.cumT, g.Dret = sb("cumT", [16, NR * P]), sb("Dret", [P, HEADS, P])
            g.SB, g.SBr = sb("SB", [P, NT + 1, W_]), sb("SBr", [HD, NT + 1, W_])
            decay_terms(nc, g)
            backward_states(nc, g)
            forward_scan(nc, g)
        with nc.sbuf_tensor("X1", [P, NT, D], F32) as g.X:
            norm_transpose(nc, g, 1)
        with nc.sbuf_tensor("sel3", [P, 3, T], F32) as g.sel3:
            with nc.sbuf_tensor("SC", [P, NT, 2 * HEADS, NKEY], F32) as g.SC:
                expert_scores(nc, g)
                select_experts(nc, g)
            dense_gates(nc, g)
    with nc.sbuf_tensor("Y", [P, NT, D], F32) as g.Y:
        experts(nc, g)
        final_norm(nc, g)


def rope_tables():
    nf = HD // 4
    inv = np.float32(10000.0) ** (-np.arange(nf, dtype=np.float32) / np.float32(nf))
    t = np.arange(T - P)
    out = np.zeros((T, 2, 48), np.float32)
    out[:, :, 0:32] = 1.0
    for half, pos in enumerate((t // 64, t % 64)):
        ang = (pos.astype(np.float32)[:, None] * inv[None, :]).astype(np.float32)
        out[P:, half, 0:16] = out[P:, half, 16:32] = np.cos(ang.astype(np.float64))
        out[P:, half, 32:48] = np.sin(ang.astype(np.float64))
    return np.concatenate([out[:, :, 0:32].reshape(T, 64), out[:, :, 32:].reshape(T, 32)], 1)


def kernel(**inputs):
    import concourse.bacc as bacc
    from concourse.bass_utils import run_bass_kernel_spmd

    A = {k: np.asarray(v) for k, v in inputs.items()}
    f = np.ascontiguousarray
    rows = lambda a: f(np.broadcast_to(a, (P,) + a.shape))
    tok = np.arange(P)
    arrays = {
        "x_all": f(np.concatenate([A["x_prompt"][0], A["x_sample"][0]], 0)),
        "c_cols": f(np.stack([A["c_ctx"], A["c"][0]], 1).reshape(KD, P, 2).transpose(1, 0, 2)),
        "w_mod": A["w_mod"][0],
        "b_mod2": f(np.broadcast_to(A["b_mod"][0], (2, 6 * D))),
        "ln_cols": f(np.broadcast_to(np.stack([A["ln1_w"][0], A["ln2_w"][0]]).reshape(2, KD, P).transpose(2, 0, 1)[..., None],
                                     (P, 2, KD, 2))),
        "ident_d": np.eye(P, dtype=np.float32),
        "w_in": A["w_in"][0],
        "conv_w_cols": f(A["conv_w"][0].reshape(TAPS, XBC // P, P).transpose(2, 1, 0)),
        "conv_b_cols": f(A["conv_b"][0].reshape(XBC // P, P).T),
        "dt_biases": rows(np.concatenate([A["dt_bias_f"][0], A["dt_bias_b"][0]])),
        "a_logs": rows(np.concatenate([A["a_log_f"][0], A["a_log_b"][0]])),
        "ret_logits": rows(np.concatenate([A["ret_logit_f"][0], A["ret_logit_b"][0]])),
        "tri_d": f(np.stack([tok[:, None] <= tok[None], tok[:, None] >= tok[None], tok[:, None] >= 0 * tok[None]], 1).astype(np.float32)),
        "sel_d": f(np.broadcast_to(np.eye(16, dtype=np.float32)[:, :, None], (16, 16, P))),
        "mneg_d": f(np.tile(np.stack([np.where(tok[None] < tok[:, None], NEG, 0), np.where(tok[None] >= tok[:, None], NEG, 0)], 1)
                            .astype(np.float32), (1, 1, 4))),
        "rope_d": rope_tables(),
        "ssd_fwd_T": f(A["state_ssd_fwd"][0, 0].transpose(2, 0, 1).reshape(P, W_)),
        "ssd_bwd_T": f(A["state_ssd_bwd"][0, 0].transpose(2, 0, 1).reshape(P, W_)),
        "ret_fwd_T": f(A["state_ret_fwd"][0, 0].transpose(2, 0, 1).reshape(HD, W_)),
        "ret_bwd_T": f(A["state_ret_bwd"][0, 0].transpose(2, 0, 1).reshape(HD, W_)),
        "skip_row": f(np.repeat(A["d_skip"][0], HD)),
        "ssm_w": A["ssm_norm_w"][0],
        "gn_w": A["ret_gn_w"][0],
        "gn_b": A["ret_gn_b"][0],
        "w_out": A["w_out"][0],
        "peer_wq": A["peer_wq"][0],
        "keys_T": f(A["peer_keys"][0].reshape(2 * HEADS, NKEY, P).transpose(2, 0, 1)),
        "iota_d": f(np.broadcast_to(np.arange(P, dtype=np.float32), (P, P))),
        "u_T": f(A["peer_u"][0].reshape(NKEY, NKEY, KD, P).transpose(1, 3, 2, 0)),
        "peer_v": A["peer_v"][0].reshape(NKEY, NKEY, D),
        "lnf": A["lnf_w"],
    }
    nc = bacc.Bacc("TRN2", target_bir_lowering=False, num_devices=1)
    g = Ctx()
    for name, a in arrays.items():
        g.__dict__[name] = nc.dram_tensor(name, a.shape, mybir.dt.from_np(a.dtype), kind="ExternalInput").ap()
    scratch = {"mod_d": (2, 6 * D), "xbc_d": (XBC, T), "tok_d": (T, TC), "rec_d": (T, REC), "x1_d": (T, D),
               "h2T_d": (P, KD, T), "gates_d": (NKEY, P, T)}
    for name, shape in scratch.items():
        g.__dict__[name] = nc.dram_tensor(name, shape, F32, kind="Internal").ap()
    outs = {"y_all": (T, D), "ssd_f_out": (P, W_), "ssd_b_out": (P, W_), "ret_f_out": (HD, W_), "ret_b_out": (HD, W_)}
    for name, shape in outs.items():
        g.__dict__[name] = nc.dram_tensor(name, shape, F32, kind="ExternalOutput").ap()
    with ExitStack() as ctx:
        program(nc, g, ctx)
    r = run_bass_kernel_spmd(nc, [arrays], core_ids=[0]).results[0]
    y = r["y_all"]
    turn = lambda a: f(a.reshape(-1, HEADS, HD).transpose(1, 2, 0)[None, None])
    return (f(y[None, :P]), f(y[None, P:]), turn(r["ssd_f_out"]), turn(r["ssd_b_out"]), turn(r["ret_f_out"]), turn(r["ret_b_out"]))
```

```python
from contextlib import ExitStack

import numpy as np

import concourse.bass as bass
from concourse import mybir

F32 = mybir.dt.float32
F32R = mybir.dt.float32r
U32 = mybir.dt.uint32
ALU = mybir.AluOpType
ACT = mybir.ActivationFunctionType
AXX = mybir.AxisListType.X

P = 128
D = 1024
KD = D // P
NT = 9
T = NT * P
GT = 2
DENSE = NT - GT
TE = DENSE * P
HEADS = 8
HD = 64
W_ = HEADS * HD
XBC = 1024
TAPS = 5
PROJ = 3600
REST0 = 512 + XBC + 16
TC = PROJ - XBC
EPS = 1e-6
NKEY = 128
TOPK = 16
NSEL = HEADS * TOPK
NEG = -1e30
LOW = -3.0e38


class Chain:

    def __init__(self, eng, sem):
        self.eng, self.sem, self.base, self.n, self.per = eng, sem, 0, 0, None

    def step(self, n):
        if isinstance(n, int) and n == 0:
            self.n = 0
            return
        if self.per is None:
            self.per = self.n
        assert self.n == self.per
        self.base, self.n = n * self.per, 0

    def link(self, ins):
        ins.then_inc(self.sem, 1)
        self.n += 1
        self.eng.wait_ge(self.sem, self.base + self.n)


class Ctx:
    pass


def new_sem(nc, ctx, name, sems):
    sems.append(ctx.enter_context(nc.semaphore(name)))
    return sems[-1]


def clear_sems(nc, sems):
    nums = sorted(s.num for s in sems)
    with nc.Block() as block:
        @block.gpsimd
        def _(pool):
            first = nums[0]
            for a, b in zip(nums, nums[1:] + [None]):
                if b != a + 1:
                    pool.sem_clear(range(first, a + 1))
                    first = b


def bcast_rows(row, n=P):
    return bass.AP(tensor=row.tensor, offset=row.offset, ap=[[0, n]] + list(row.ap)[-1:])


def modulation(nc, g):
    GW = 512
    NG = 6 * D // GW
    with ExitStack() as ctx:
        sb = lambda n, s, d=F32: ctx.enter_context(nc.sbuf_tensor(n, s, d))
        sems = []
        sem = lambda n: new_sem(nc, ctx, n, sems)
        cT, cs = sb("cT", [P, KD, 2]), sb("cs", [P, KD, 2])
        wm = [sb(f"wm{i}", [P, KD, GW]) for i in range(3)]
        bm, row = sb("bmod", [2, 6 * D]), sb("modrow", [2, 6 * D])
        lnc = sb("lnc", [P, 2, KD, 2])
        small, x_loaded, row_stored = sem("mod_small"), sem("mod_x"), sem("mod_stored")
        w_loaded = [sem(f"mod_w{i}") for i in range(3)]
        silu_done, group_done, row_done = sem("mod_silu"), sem("mod_group"), sem("mod_row")
        cols_done, chain_sem = sem("mod_cols"), sem("mod_chain")
        wv = g.w_mod.rearrange("(k p) n -> p k n", p=P)
        ctx.callback(clear_sems, nc, sems)
        block = ctx.enter_context(nc.Block())

        @block.sync
        def _(sp):
            for dst, src in ((cT[:], g.c_cols), (bm[:], g.b_mod2), (lnc[:], g.ln_cols), (g.ident[:], g.ident_d)):
                sp.dma_start(dst, src).then_inc(small, 16)
            for n in range(3):
                sp.dma_start(wm[n][:], wv[:, :, n * GW:(n + 1) * GW]).then_inc(w_loaded[n], 16)
            with sp.Fori(1, NG // 3) as i:
                for s in range(3):
                    sp.wait_ge(group_done, i * 3 + (s - 2))
                    sp.dma_start(wm[s][:], wv[:, :, bass.ds(i * (3 * GW) + s * GW, GW)]).then_inc(w_loaded[s], 16)
            sp.dma_start(g.X[:], g.x_all.rearrange("(t p) d -> p t d", p=P)).then_inc(x_loaded, 16)
            sp.wait_ge(row_done, NG + 3)
            sp.dma_start(g.mod_d, row[:]).then_inc(row_stored, 16)
            sp.wait_ge(row_stored, 16)
            sp.wait_ge(x_loaded, 16)

        @block.scalar
        def _(act):
            act.wait_ge(small, 64)
            act.activation(cs[:], cT[:], ACT.Silu).then_inc(silu_done, 1)

        @block.tensor
        def _(pe):
            pe.wait_ge(silu_done, 1)
            with pe.Fori(0, NG // 3) as i:
                for s in range(3):
                    pe.wait_ge(w_loaded[s], i * 16 + 16)
                    pe.wait_ge(row_done, i * 3 + s + 1)
                    for k in range(KD):
                        mm = pe.matmul(g.ps[s][0:2, :], cs[:, k, :], wm[s][:, k, :], start=(k == 0), stop=(k == KD - 1))
                    mm.then_inc(group_done, 1)
            pe.wait_ge(row_done, NG + 3)
            for v, col in enumerate((0, 1, 3, 4)):
                for k in range(KD):
                    c = (v * KD + k) * 2
                    mm = pe.matmul(g.ps[3][:, c:c + 2], row[0:2, col * D + k * P:col * D + (k + 1) * P],
                                   g.ident[0:2, 0:2], start=True, stop=True)
            mm.then_inc(cols_done, 1)

        @block.vector
        def _(dve):
            own = Chain(dve, chain_sem)
            dve.sem_inc(row_done, 3)
            dve.wait_ge(small, 64)
            with dve.Fori(0, NG // 3) as i:
                for s in range(3):
                    dve.wait_ge(group_done, i * 3 + s + 1)
                    cols = bass.ds(i * (3 * GW) + s * GW, GW)
                    dve.tensor_tensor(row[:, cols], g.ps[s][0:2, :], bm[:, cols], ALU.add).then_inc(row_done, 1)
            dve.wait_ge(cols_done, 1)
            m = g.ps[3][:, 0:4 * KD * 2].rearrange("p (v k s) -> p v k s", v=4, k=KD)
            for v in range(2):
                own.link(dve.tensor_copy(g.shift[:, v], m[:, 2 * v]))
                own.link(dve.scalar_tensor_tensor(g.gain[:, v], m[:, 2 * v + 1], 1.0, lnc[:, v], ALU.add, ALU.mult))


def norm_transpose(nc, g, v):
    with ExitStack() as ctx:
        sb = lambda n, s, d=F32: ctx.enter_context(nc.sbuf_tensor(n, s, d))
        sems = []
        sem = lambda n: new_sem(nc, ctx, f"nt{v}_{n}", sems)
        xn = [sb(f"xn{v}{i}", [P, D]) for i in range(2)]
        junk = sb(f"ntjunk{v}", [P, D])
        ss, rs = sb(f"ntss{v}", [P, NT]), sb(f"ntrs{v}", [P, NT])
        chain_sem, ms_ready, root_done, rstd_ready = sem("chain"), sem("ms"), sem("root"), sem("rstd")
        xn_ready, xn_free, turned, banks_free_a, banks_free_v = (
            sem("xn"), sem("xnfree"), sem("turned"), sem("bfa"), sem("bfv"))
        ctx.callback(clear_sems, nc, sems)
        block = ctx.enter_context(nc.Block())
        H = KD // 2
        x_loaded, wq_loaded = [sem(f"x{i}") for i in range(3)], sem("wq")

        @block.sync
        def _(sp):
            if v == 1:
                xv = g.x1_d.rearrange("(t p) d -> p t d", p=P)
                for i in range(3):
                    sp.dma_start(g.X[:, 3 * i:3 * i + 3], xv[:, 3 * i:3 * i + 3]).then_inc(x_loaded[i], 16)
                sp.dma_start(g.wq[:], g.peer_wq.rearrange("(k p) n -> p k n", p=P)).then_inc(wq_loaded, 16)
                sp.wait_ge(wq_loaded, 16)

        def tiles(eng, body):
            body(0, 0, 0)
            with eng.Fori(0, (NT - 1) // 2) as i:
                body(i * 2 + 1, 1, 1)
                body(i * 2 + 2, 0, 1)

        @block.scalar
        def _(act):
            act.sem_inc(banks_free_a, 2)
            act.wait_ge(ms_ready, 1)
            act.activation(rs[:], ss[:], ACT.Sqrt).then_inc(root_done, 1)

            def body(t, s, seq):
                act.wait_ge(turned, t + 1)
                for k in range(H):
                    a = act.activation(g.hT[:, k, bass.ds(t * P, P)], g.ps[4 * s + k // 4][:, (k % 4) * P:(k % 4 + 1) * P],
                                       ACT.Identity, bias=g.shift[:, v, k, seq:seq + 1], scale=g.gain[:, v, k, seq:seq + 1])
                a.then_inc(banks_free_a, 1)
            tiles(act, body)

        @block.vector
        def _(dve):
            own = Chain(dve, chain_sem)
            dve.sem_inc(banks_free_v, 2)
            for t in range(NT):
                if v == 1 and t % 3 == 0:
                    dve.wait_ge(x_loaded[t // 3], 16)
                own.link(dve.tensor_tensor_reduce(junk[:], g.X[:, t, :], g.X[:, t, :], 1.0, 0.0, ALU.mult, ALU.add,
                                                  ss[:, t:t + 1]))
            own.link(dve.tensor_scalar(ss[:], ss[:], 1.0 / D, EPS, ALU.mult, ALU.add))
            dve.sem_inc(ms_ready, 1)
            dve.wait_ge(root_done, 1)
            own.link(dve.reciprocal(rs[:], rs[:]))

            def scale(t, s):
                dve.wait_ge(xn_free, t + 1)
                dve.tensor_scalar(xn[s][:], g.X[:, t, :], rs[:, bass.ds(t, 1)], None, ALU.mult).then_inc(xn_ready, 1)

            def evac(t, s, seq):
                dve.wait_ge(turned, t + 1)
                for k in range(H, KD):
                    a = dve.tensor_scalar(g.hT[:, k, bass.ds(t * P, P)], g.ps[4 * s + k // 4][:, (k % 4) * P:(k % 4 + 1) * P],
                                          g.gain[:, v, k, seq:seq + 1], g.shift[:, v, k, seq:seq + 1], ALU.mult, ALU.add)
                a.then_inc(banks_free_v, 1)

            scale(0, 0)
            scale(1, 1)
            evac(0, 0, 0)
            with dve.Fori(0, (NT - 1) // 2 - 1) as i:
                scale(i * 2 + 2, 0)
                evac(i * 2 + 1, 1, 1)
                scale(i * 2 + 3, 1)
                evac(i * 2 + 2, 0, 1)
            scale(NT - 1, 0)
            evac(NT - 2, 1, 1)
            evac(NT - 1, 0, 1)

        @block.tensor
        def _(pe):
            pe.sem_inc(xn_free, 2)

            def body(t, s, seq):
                pe.wait_ge(xn_ready, t + 1)
                pe.wait_ge(banks_free_a, t + 1)
                pe.wait_ge(banks_free_v, t + 1)
                for k in range(KD):
                    mm = pe.transpose(g.ps[4 * s + k // 4][:, (k % 4) * P:(k % 4 + 1) * P], xn[s][:, k * P:(k + 1) * P],
                                      g.ident[:])
                mm.then_inc(turned, 1)
                pe.wait_ge(turned, t + 1)
                pe.sem_inc(xn_free, 1)
            tiles(pe, body)


def project_in(nc, g):
    PAD = TAPS // 2
    WID = T + 4 * PAD
    LAT = P + 2 * PAD
    TG = 384
    NB = XBC // P
    NQ = 3
    with ExitStack() as ctx:
        sb = lambda n, s, d=F32: ctx.enter_context(nc.sbuf_tensor(n, s, d))
        sems = []
        sem = lambda n: new_sem(nc, ctx, f"pi_{n}", sems)
        wx = [sb(f"wx{i}", [P, KD, P]) for i in range(2)]
        pre = [sb(f"pre{i}", [P, WID]) for i in range(2)]
        acc = [sb(f"acc{i}", [P, WID - 2 * PAD]) for i in range(2)]
        cv = [sb(f"cv{i}", [P, T]) for i in range(2)]
        cw, cb = sb("cw", [P, NB, TAPS]), sb("cb", [P, NB])
        wt = [sb(f"wt{i}", [P, KD, 512]) for i in range(2)]
        wd, dts = sb("wdt", [P, KD, 16]), sb("dts", [P, NT, 16])
        st = [sb(f"st{i}", [P, 512]) for i in range(NQ)]
        small, wd_loaded, padded, chain_sem, chain_sem_v = sem("small"), sem("wd"), sem("padded"), sem("chain"), sem("chainv")
        wx_loaded, wt_loaded = [sem("wx0"), sem("wx1")], [sem("wt0"), sem("wt1")]
        block_done, banks_free, pre_ready, pre_free = sem("block"), sem("banksfree"), sem("pre"), sem("prefree")
        conv_done, acc_free, silu_done = sem("conv"), sem("accfree"), sem("silu")
        cv_stored = [sem("cvst0"), sem("cvst1")]
        dt_done, dt_copied, dt_stored = sem("dt"), sem("dtcopied"), sem("dtstored")
        tile_done, tile_copied, group_done = sem("tile"), sem("tilecopied"), sem("group")
        st_stored = [sem(f"st{i}") for i in range(NQ)]
        wv = g.w_in.rearrange("(k p) n -> p k n", p=P)
        ctx.callback(clear_sems, nc, sems)
        block = ctx.enter_context(nc.Block())

        def groups(eng, body):
            body(0, 0)
            with eng.Fori(0, 2) as i:
                body(i * 2 + 1, 1)
                body(i * 2 + 2, 0)

        @block.gpsimd
        def _(pool):
            for s in range(2):
                for a, b in ((0, PAD), (PAD + P, 3 * PAD + P), (WID - PAD, WID)):
                    pool.memset(pre[s][:, a:b], 0.0).then_inc(padded, 1)
            pool.dma_start(cw[:], g.conv_w_cols).then_inc(small, 16)
            pool.dma_start(cb[:], g.conv_b_cols).then_inc(small, 16)
            for s in range(2):
                pool.dma_start(wx[s][:], wv[:, :, 512 + s * P:512 + (s + 1) * P]).then_inc(wx_loaded[s], 16)
            pool.dma_start(wd[:], wv[:, :, 512 + XBC:REST0]).then_inc(wd_loaded, 16)
            pool.dma_start(wt[0][:], wv[:, :, 0:512]).then_inc(wt_loaded[0], 16)
            pool.dma_start(wt[1][:], wv[:, :, REST0:REST0 + 512]).then_inc(wt_loaded[1], 16)
            with pool.Fori(0, NB // 2 - 1) as i:
                for s in range(2):
                    pool.wait_ge(block_done, i * 2 + s + 1)
                    pool.dma_start(wx[s][:], wv[:, :, bass.ds(i * (2 * P) + (512 + (2 + s) * P), P)]).then_inc(wx_loaded[s], 16)
            for j in range(3):
                pool.wait_ge(group_done, j + 1)
                c = REST0 + (j + 1) * 512
                pool.dma_start(wt[j % 2][:], wv[:, :, c:c + 512]).then_inc(wt_loaded[j % 2], 16)

        @block.sync
        def _(sp):
            for s in range(2):
                sp.sem_inc(cv_stored[s], 16)
            for s in range(NQ):
                sp.sem_inc(st_stored[s], 16)
            with sp.Fori(0, NB // 2) as i:
                for s in range(2):
                    sp.wait_ge(silu_done, i * 2 + s + 1)
                    sp.dma_start(g.xbc_d[bass.ds(i * (2 * P) + s * P, P), :], cv[s][:]).then_inc(cv_stored[s], 16)
            sp.wait_ge(dt_copied, 1)
            sp.dma_start(g.tok_d[:, 5 * 512:].rearrange("(t p) c -> p t c", p=P), dts[:]).then_inc(dt_stored, 16)

            def store(grp, s):
                for t in range(NT):
                    sp.wait_ge(tile_copied, grp * NT + t + 1)
                    sp.dma_start(g.tok_d[t * P:(t + 1) * P, bass.ds(grp * 512, 512)], st[t % NQ][:]).then_inc(st_stored[t % NQ], 16)
            groups(sp, store)
            for s in range(2):
                sp.wait_ge(cv_stored[s], 16 * (NB // 2 + 1))
            sp.wait_ge(dt_stored, 16)
            for s in range(NQ):
                sp.wait_ge(st_stored[s], 16 * (5 * NT // NQ + 1))

        @block.tensor
        def _(pe):
            with pe.Fori(0, NB // 2) as i:
                for s in range(2):
                    pe.wait_ge(wx_loaded[s], i * 16 + 16)
                    pe.wait_ge(banks_free, i * 2 + s + 1)
                    for q in range(T // TG):
                        for k in range(KD):
                            mm = pe.matmul(g.ps[3 * s + q][:, 0:TG], wx[s][:, k, :], g.hT[:, k, q * TG:(q + 1) * TG],
                                           start=(k == 0), stop=(k == KD - 1))
                    mm.then_inc(block_done, 1)
            pe.wait_ge(wd_loaded, 16)
            for t in range(NT):
                for k in range(KD):
                    mm = pe.matmul(g.ps[6][:, 16 * t:16 * t + 16], g.hT[:, k, t * P:(t + 1) * P], wd[:, k, :],
                                   start=(k == 0), stop=(k == KD - 1))
            mm.then_inc(dt_done, 1)
            pe.wait_ge(banks_free, NB + 2)

            def group(grp, s):
                pe.wait_ge(wt_loaded[s], (grp // 2) * 16 + 16)
                for t in range(NT):
                    if not (isinstance(grp, int) and t < NQ):
                        pe.wait_ge(tile_copied, grp * NT + (t - NQ + 1))
                    for k in range(KD):
                        mm = pe.matmul(g.ps[t % NQ][:], g.hT[:, k, t * P:(t + 1) * P], wt[s][:, k, :],
                                       start=(k == 0), stop=(k == KD - 1))
                    mm.then_inc(tile_done, 1)
                pe.wait_ge(tile_done, grp * NT + NT)
                pe.sem_inc(group_done, 1)
            groups(pe, group)

        @block.scalar
        def _(act):
            act.sem_inc(banks_free, 2)
            act.wait_ge(padded, 6)
            act.wait_ge(small, 32)

            def copy_in(n, s, i):
                act.wait_ge(block_done, n + 1)
                act.wait_ge(pre_free, n + 1)
                act.activation(pre[s][:, PAD:PAD + P], g.ps[3 * s][:, 0:P], ACT.Copy)
                act.activation(pre[s][:, 3 * PAD + P:3 * PAD + TG], g.ps[3 * s][:, P:TG], ACT.Copy)
                for q in range(1, T // TG):
                    z = act.activation(pre[s][:, 3 * PAD + q * TG:3 * PAD + (q + 1) * TG], g.ps[3 * s + q][:, 0:TG], ACT.Copy)
                z.then_inc(pre_ready, 1)
                act.wait_ge(pre_ready, n + 1)
                act.sem_inc(banks_free, 1)

            def silu(n, s, i):
                act.wait_ge(conv_done, n + 1)
                act.wait_ge(cv_stored[s], i * 16 + 16)
                act.activation(cv[s][:, 0:P], acc[s][:, 0:P], ACT.Silu, bias=cb[:, bass.ds(n, 1)]).then_inc(chain_sem, 1)
                act.activation(cv[s][:, P:T], acc[s][:, LAT:LAT + T - P], ACT.Silu, bias=cb[:, bass.ds(n, 1)]).then_inc(chain_sem, 1)
                act.wait_ge(chain_sem, n * 2 + 2)
                act.sem_inc(silu_done, 1)
                act.sem_inc(acc_free, 1)
            with act.Fori(0, NB // 2) as i:
                for s in range(2):
                    copy_in(i * 2 + s, s, i)
                    silu(i * 2 + s, s, i)
            act.wait_ge(dt_done, 1)
            act.activation(dts[:], g.ps[6][:, 0:16 * NT].rearrange("p (t c) -> p t c", t=NT), ACT.Copy).then_inc(dt_copied, 1)

            def group(grp, s):
                for t in range(NT):
                    act.wait_ge(tile_done, grp * NT + t + 1)
                    act.wait_ge(st_stored[t % NQ], grp * (16 * NT // NQ) + (t // NQ) * 16 + 16)
                    act.activation(st[t % NQ][:], g.ps[t % NQ][:], ACT.Copy).then_inc(tile_copied, 1)
            groups(act, group)

        @block.vector
        def _(dve):
            dve.sem_inc(pre_free, 2)
            dve.sem_inc(acc_free, 2)
            dve.wait_ge(small, 32)
            with dve.Fori(0, NB // 2) as i:
                for s in range(2):
                    n = i * 2 + s
                    dve.wait_ge(pre_ready, n + 1)
                    dve.wait_ge(acc_free, n + 1)
                    N = WID - 2 * PAD
                    for tap in range(TAPS):
                        w = cw[:, bass.ds(n, 1), tap]
                        x = pre[s][:, tap:tap + N]
                        if tap == 0:
                            z = dve.tensor_scalar(acc[s][:], x, w, None, ALU.mult)
                        else:
                            z = dve.scalar_tensor_tensor(acc[s][:], x, w, acc[s][:], ALU.mult, ALU.add)
                        z.then_inc(chain_sem_v, 1)
                        dve.wait_ge(chain_sem_v, n * TAPS + tap + 1)
                    dve.sem_inc(conv_done, 1)
                    dve.sem_inc(pre_free, 1)


NR = NT + 1
RSC = HD ** -0.5


def decay_terms(nc, g):
    with ExitStack() as ctx:
        sb = lambda n, s, d=F32: ctx.enter_context(nc.sbuf_tensor(n, s, d))
        sems = []
        sem = lambda n: new_sem(nc, ctx, f"dc_{n}", sems)
        x, u, w, l, c, m = (sb(f"dc{n}", [P, NR, 16]) for n in "xuwlcm")
        bias, alog, la = sb("dcbias", [P, 16]), sb("dcalog", [P, 16]), sb("dcla", [P, NR, 16])
        cum, tri = sb("cum", [P, NR, 16]), sb("tri", [P, 3, P])
        ef, eb = sb("ef", [P, HEADS, P]), sb("eb", [P, HEADS, P])
        loaded, x_ready, u_ready, w_ready, l_ready, a_ready = (sem(n) for n in ("ld", "x", "u", "w", "l", "a"))
        la_ready, sums_done, cum_ready, exps_done, turned, cumT_ready, seg_done, seg_exp = (
            sem(n) for n in ("la", "sums", "cum", "exps", "turned", "cumT", "seg", "segexp"))
        chain = sem("chain")
        ctx.callback(clear_sems, nc, sems)
        block = ctx.enter_context(nc.Block())

        @block.sync
        def _(sp):
            for dst, src in ((x[:, 0:NT, :], g.tok_d[:, 5 * 512:].rearrange("(t p) c -> p t c", p=P)),
                             (x[:, NT, :], g.ret_logits), (bias[:], g.dt_biases), (alog[:], g.a_logs),
                             (tri[:], g.tri_d), (g.sel[:], g.sel_d), (g.mneg[:], g.mneg_d)):
                sp.dma_start(dst, src).then_inc(loaded, 16)

        @block.scalar
        def _(act):
            act.wait_ge(loaded, 7 * 16)
            act.activation(alog[:], alog[:], ACT.Exp).then_inc(a_ready, 1)
            act.wait_ge(x_ready, 1)
            act.activation(u[:], m[:], ACT.Exp).then_inc(u_ready, 1)
            act.wait_ge(w_ready, 1)
            act.activation(l[:], w[:], ACT.Ln).then_inc(l_ready, 1)
            act.wait_ge(cum_ready, 1)
            act.activation(g.EC[:], cum[:], ACT.Exp).then_inc(exps_done, 1)
            act.activation(g.WD[:], c[:], ACT.Exp).then_inc(exps_done, 1)
            act.activation(g.CD[:], g.ps[2][:, 0:16 * NR].rearrange("p (r c) -> p r c", r=NR), ACT.Exp).then_inc(exps_done, 1)
            act.wait_ge(turned, 1)
            for r in range(NR):
                z = act.activation(g.cumT[:, r * P:(r + 1) * P], g.ps[4 + r // 4][0:16, (r % 4) * P:(r % 4 + 1) * P], ACT.Copy)
            z.then_inc(cumT_ready, 1)
            act.wait_ge(seg_done, 1)
            for h in range(16):
                e = ef if h < 8 else eb
                z = act.activation(e[:, h % 8, :], g.ps[h // 4][:, (h % 4) * P:(h % 4 + 1) * P], ACT.Exp,
                                   bias=g.NC[:, NT, h:h + 1])
            z.then_inc(seg_exp, 1)

        @block.vector
        def _(dve):
            own = Chain(dve, chain)
            dve.wait_ge(loaded, 7 * 16)
            own.link(dve.tensor_tensor(x[:, 0:NT], x[:, 0:NT], bias[:].unsqueeze(1).broadcast_to([P, NT, 16]), ALU.add))
            own.link(dve.tensor_scalar(x[:, NT], x[:, NT], -1.0, None, ALU.mult))
            own.link(dve.scalar_tensor_tensor(m[:], x[:], -1.0, x[:], ALU.mult, ALU.min))
            dve.sem_inc(x_ready, 1)
            dve.wait_ge(u_ready, 1)
            own.link(dve.tensor_scalar(w[:], u[:], 1.0, None, ALU.add))
            dve.sem_inc(w_ready, 1)
            own.link(dve.tensor_scalar(c[:], w[:], 1.0, None, ALU.subtract))
            own.link(dve.scalar_tensor_tensor(m[:], c[:], 0.0, u[:], ALU.is_equal, ALU.mult))
            own.link(dve.tensor_scalar(c[:], c[:], 1e-30, None, ALU.max))
            own.link(dve.reciprocal(c[:], c[:]))
            own.link(dve.tensor_tensor(c[:], c[:], u[:], ALU.mult))
            dve.wait_ge(l_ready, 1)
            own.link(dve.tensor_tensor(c[:], c[:], l[:], ALU.mult))
            own.link(dve.tensor_tensor(c[:], c[:], m[:], ALU.add))
            own.link(dve.scalar_tensor_tensor(g.DT[:], x[:], 0.0, c[:], ALU.max, ALU.add))
            dve.wait_ge(a_ready, 1)
            own.link(dve.tensor_tensor(la[:, 0:NT], g.DT[:, 0:NT], alog[:].unsqueeze(1).broadcast_to([P, NT, 16]), ALU.mult))
            own.link(dve.tensor_scalar(la[:, 0:NT], la[:, 0:NT], -1.0, None, ALU.mult))
            own.link(dve.tensor_scalar(la[:, NT], g.DT[:, NT], -1.0, None, ALU.mult))
            dve.sem_inc(la_ready, 1)
            dve.wait_ge(sums_done, 1)
            for d in range(2):
                own.link(dve.tensor_copy(cum[:, :, 8 * d:8 * d + 8], g.ps[d][:, 0:8 * NR].rearrange("p (r c) -> p r c", r=NR)))
            own.link(dve.tensor_scalar(g.NC[:], cum[:], -1.0, None, ALU.mult))
            own.link(dve.tensor_tensor(c[:], g.ps[2][:, 0:16 * NR].rearrange("p (r c) -> p r c", r=NR), cum[:], ALU.subtract))
            dve.sem_inc(cum_ready, 1)
            dve.wait_ge(exps_done, 3)
            own.link(dve.tensor_tensor(g.WD[:, 0:NT], g.WD[:, 0:NT], g.DT[:, 0:NT], ALU.mult))
            own.link(dve.tensor_scalar(g.WD[:, NT], g.WD[:, NT], RSC, None, ALU.mult))
            dve.wait_ge(seg_exp, 1)
            own.link(dve.tensor_tensor(ef[:], ef[:], eb[:], ALU.add))
            own.link(dve.tensor_scalar(g.Dret[:], ef[:], RSC, None, ALU.mult))

        @block.tensor
        def _(pe):
            pe.wait_ge(la_ready, 1)
            pe.matmul(g.ps[0][:, 0:8 * NR], tri[:, 0, :], la[:, :, 0:8], start=True, stop=True)
            pe.matmul(g.ps[1][:, 0:8 * NR], tri[:, 1, :], la[:, :, 8:16], start=True, stop=True)
            pe.matmul(g.ps[2][:, 0:16 * NR], tri[:, 2, :], la[:], start=True, stop=True).then_inc(sums_done, 1)
            pe.wait_ge(cum_ready, 1)
            for r in range(NR):
                mm = pe.transpose(g.ps[4 + r // 4][0:16, (r % 4) * P:(r % 4 + 1) * P], cum[:, r, :], g.ident[:])
            mm.then_inc(turned, 1)
            pe.wait_ge(cumT_ready, 1)
            pe.wait_ge(exps_done, 3)
            seg = None
            for q in range(4):
                seg = segment(pe, g, q, g.ps[q], NT)
            seg.then_inc(seg_done, 1)


def segment(pe, g, q, bank, r):
    mm = pe.matmul(bank[:], g.ident[:], g.mneg[:, q // 2], start=True, stop=False, skip_group_check=True)
    for h in range(4):
        mm = pe.matmul(bank[:, h * P:(h + 1) * P], g.sel[:, 4 * q + h, :], g.cumT[:, bass.ds(r * P, P)],
                       start=False, stop=(h == 3), skip_group_check=True)
    return mm


def heads_bcast(ap):
    return ap.unsqueeze(2).broadcast_to([ap.shape[0], HEADS, HD])


REC = W_ + 2 * P + 2 * W_


def backward_states(nc, g):
    with ExitStack() as ctx:
        sb = lambda n, s, d=F32: ctx.enter_context(nc.sbuf_tensor(n, s, d))
        sems = []
        sem = lambda n: new_sem(nc, ctx, f"bw_{n}", sems)
        tk = [sb(f"bwtk{i}", [P, 3 * W_]) for i in range(2)]
        xb = [sb(f"bwxb{i}", [P, 6, P]) for i in range(2)]
        rec = [sb(f"bwrec{i}", [P, REC]) for i in range(2)]
        rt, rp = sb("bwrt", [P, 2 * W_]), sb("bwrp", [P, 2 * W_])
        rope = sb("rope", [P, NT, 96])
        xw, vw = sb("bwxw", [P, W_]), sb("bwvw", [P, W_])
        tmp, tmpr = sb("bwtmp", [P, W_]), sb("bwtmpr", [HD, W_])
        small, zeroed, loaded = sem("small"), sem("zeroed"), [sem("ld0"), sem("ld1")]
        turned, x_copied, k_ready, xw_ready, vw_ready, states_done, state_ready = (
            sem(n) for n in ("turned", "xcopied", "k", "xw", "vw", "states", "state"))
        rec_stored, out_stored, chain = [sem("rec0"), sem("rec1")], sem("out"), sem("chain")
        ctx.callback(clear_sems, nc, sems)
        block = ctx.enter_context(nc.Block())

        def steps(eng, body):
            body(0, 0, 0, 0, 1)
            with eng.Fori(0, (NT - 1) // 2) as i:
                for s in (1, 0):
                    tile = eng.snap(i * -2 + (7 + s))
                    body(i * 2 + (2 - s), s, tile, tile + 1, tile)

        @block.sync
        def _(sp):
            sp.dma_start(rope[:], g.rope_d.rearrange("(t p) c -> p t c", p=P)).then_inc(small, 16)
            sp.dma_start(g.SB[:, NT, :], g.ssd_bwd_T).then_inc(small, 16)
            sp.dma_start(g.SBr[:, NT, :], g.ret_bwd_T).then_inc(small, 16)
            sp.sem_inc(rec_stored[0], 16)
            sp.sem_inc(rec_stored[1], 16)
            sp.sem_inc(state_ready, 2)

            def load(n, s, t, a, b):
                sp.wait_ge(state_ready, n + 1)
                rows = bass.ds(t * P, P)
                sp.dma_start(tk[s][:], g.tok_d[rows, W_:4 * W_]).then_inc(loaded[s], 16)
                sp.dma_start(xb[s][:], g.xbc_d[0:6 * P, :].rearrange("(c p) t -> p c t", p=P)[:, :, rows]).then_inc(loaded[s], 16)
            steps(sp, load)

        @block.scalar
        def _(act):
            def copy(n, s, t, a, b):
                act.wait_ge(turned, n + 1)
                act.wait_ge(rec_stored[s], ((n // 2) * 16 + 16))
                act.activation(rec[s][:, 0:W_], g.ps[0][:], ACT.Copy)
                act.activation(rec[s][:, W_:W_ + 2 * P], g.ps[1][:, 0:2 * P], ACT.Copy).then_inc(x_copied, 1)
                act.wait_ge(x_copied, n + 1)
                act.wait_ge(k_ready, n + 1)
                act.dma_start(g.rec_d[bass.ds(t * P, P), :], rec[s][:]).then_inc(rec_stored[s], 16)
                if isinstance(n, int):
                    act.wait_ge(state_ready, n + 3)
                    act.dma_start(g.ssd_b_out, g.SB[:, b, :]).then_inc(out_stored, 16)
                    act.dma_start(g.ret_b_out, g.SBr[:, b, :]).then_inc(out_stored, 16)
            steps(act, copy)
            act.wait_ge(out_stored, 32)
            act.wait_ge(rec_stored[0], 16 * 6)
            act.wait_ge(rec_stored[1], 16 * 5)

        @block.gpsimd
        def _(pool):
            pool.memset(g.SB[:, 0, :], 0.0).then_inc(zeroed, 1)
            pool.memset(g.SBr[:, 0, :], 0.0).then_inc(zeroed, 1)

            def weigh(n, s, t, a, b):
                pool.wait_ge(loaded[s], (n // 2) * 32 + 32)
                pool.wait_ge(state_ready, n + 2)
                pool.tensor_tensor(vw[:].rearrange("p (h d) -> p h d", h=HEADS), tk[s][:, 2 * W_:].rearrange("p (h d) -> p h d", h=HEADS),
                                   heads_bcast(g.WD[:, NT, 8:16]), ALU.mult).then_inc(vw_ready, 1)
            steps(pool, weigh)

        @block.vector
        def _(dve):
            own = Chain(dve, chain)
            dve.wait_ge(small, 48)
            dve.wait_ge(zeroed, 2)

            def step(n, s, t, a, b):
                own.step(n)
                dve.wait_ge(loaded[s], (n // 2) * 32 + 32)
                dve.wait_ge(rec_stored[s], (n // 2) * 16 + 16)
                qk = tk[s][:, 0:2 * W_]
                v4 = lambda ap, i: ap.rearrange("p (h f i c) -> p h f i c", f=2, i=2, c=16)[:, :, :, i, :]
                sin = rope[:, bass.ds(t, 1), 64:96].rearrange("p o (f c) -> p (o f) c", f=2).unsqueeze(1).broadcast_to([P, 16, 2, 16])
                dve.tensor_tensor(rp[:].rearrange("p (h c) -> p h c", c=HD), qk.rearrange("p (h c) -> p h c", c=HD),
                                  rope[:, bass.ds(t, 1), 0:64].broadcast_to([P, 16, HD]), ALU.mult)
                own.link(dve.tensor_tensor(v4(rt[:], 0), v4(qk, 1), sin, ALU.mult))
                own.link(dve.tensor_tensor(v4(rt[:], 1), v4(qk, 0), sin, ALU.mult))
                out = rec[s][:, W_ + 2 * P:REC]
                own.link(dve.tensor_tensor(v4(out, 0), v4(rp[:], 0), v4(rt[:], 0), ALU.subtract))
                own.link(dve.tensor_tensor(v4(out, 1), v4(rp[:], 1), v4(rt[:], 1), ALU.add))
                dve.sem_inc(k_ready, 1)
                dve.wait_ge(x_copied, n + 1)
                dve.tensor_tensor(xw[:].rearrange("p (h d) -> p h d", h=HEADS), rec[s][:, 0:W_].rearrange("p (h d) -> p h d", h=HEADS),
                                  g.WD[:, bass.ds(t, 1), 8:16].rearrange("p o h -> p (o h)").unsqueeze(2).broadcast_to([P, HEADS, HD]),
                                  ALU.mult).then_inc(xw_ready, 1)
                own.link(dve.tensor_tensor(tmp[:].rearrange("p (h d) -> p h d", h=HEADS),
                                           g.SB[:, bass.ds(a, 1), :].rearrange("p o (h d) -> p (o h) d", h=HEADS),
                                           g.CD[:, bass.ds(t, 1), 8:16].rearrange("p o h -> p (o h)").unsqueeze(2).broadcast_to([P, HEADS, HD]),
                                           ALU.mult))
                own.link(dve.tensor_tensor(tmpr[:].rearrange("p (h d) -> p h d", h=HEADS),
                                           g.SBr[:, bass.ds(a, 1), :].rearrange("p o (h d) -> p (o h) d", h=HEADS),
                                           heads_bcast(g.CD[0:HD, NT, 8:16]), ALU.mult))
                dve.wait_ge(states_done, n + 1)
                if not isinstance(n, int):
                    dve.wait_ge(out_stored, 32)
                own.link(dve.tensor_tensor(g.SB[:, bass.ds(b, 1), :].rearrange("p o c -> p (o c)"), tmp[:], g.ps[2][:], ALU.add))
                own.link(dve.tensor_tensor(g.SBr[:, bass.ds(b, 1), :].rearrange("p o c -> p (o c)"), tmpr[:], g.ps[3][0:HD, :], ALU.add))
                dve.sem_inc(state_ready, 1)
            steps(dve, step)

        @block.tensor
        def _(pe):
            def step(n, s, t, a, b):
                pe.wait_ge(loaded[s], (n // 2) * 32 + 32)
                pe.wait_ge(state_ready, n + 2)
                for c in range(6):
                    mm = pe.transpose(g.ps[c // 4][:, (c % 4) * P:(c % 4 + 1) * P], xb[s][:, c, :], g.ident[:])
                mm.then_inc(turned, 1)
                pe.wait_ge(xw_ready, n + 1)
                for gr in range(2):
                    pe.matmul(g.ps[2][:, gr * 256:(gr + 1) * 256], rec[s][:, W_ + gr * P:W_ + (gr + 1) * P],
                              xw[:, gr * 256:(gr + 1) * 256], start=True, stop=True)
                pe.wait_ge(vw_ready, n + 1)
                pe.wait_ge(k_ready, n + 1)
                for h in range(HEADS):
                    k = rec[s][:, W_ + 2 * P + W_ + h * HD:][:, 0:HD]
                    mm = pe.matmul(g.ps[3][0:HD, h * HD:(h + 1) * HD], k, vw[:, h * HD:(h + 1) * HD], start=True, stop=True)
                mm.then_inc(states_done, 1)
            steps(pe, step)


def forward_scan(nc, g):
    with ExitStack() as ctx:
        sb = lambda n, s, d=F32: ctx.enter_context(nc.sbuf_tensor(n, s, d))
        sems = []
        sem = lambda n: new_sem(nc, ctx, f"fw_{n}", sems)
        zvg = [sb(f"zvg{i}", [P, 3 * W_]) for i in range(2)]
        bc = [sb(f"bc{i}", [P, 4, P]) for i in range(2)]
        rec = [sb(f"fwrec{i}", [P, REC]) for i in range(2)]
        qkT = sb("qkT", [HD, 16, P])
        dec = sb("dec", [P, 16, P])
        M, Mr = dec[:, 0:8, :], sb("Mr", [P, HEADS, P])
        xt = [sb(f"fwx{i}", [P, D]) for i in range(2)]
        sf, sr = sb("sf", [P, W_]), sb("sr", [HD, HEADS, 2, HD])
        sfr = sr[:, :, 0, :]
        xw, vw = sb("fwxw", [P, W_]), sb("fwvw", [P, W_])
        y, t1, t2 = sb("y", [P, W_]), sb("t1", [P, W_]), sb("t2", [P, W_])
        r, r2 = sb("r", [P, W_]), sb("r2", [P, W_])
        gate = sb("gate", [P, 2, W_])
        ycat, yT = sb("ycat", [P, 2 * W_]), sb("yT", [P, KD, P])
        st = sb("fwst", [P, 9])
        mean = sb("mean", [P, HEADS])
        skip, nw, gw, gb = (sb(f"fw{n}", [P, W_]) for n in ("skip", "nw", "gw", "gb"))
        g1 = sb("g1", [P, 2, D])
        wo, gained = g.hT[:, :, 0:D], g.hT[:, :, D:T]
        small, loaded, x_stored = sem("small"), [sem("ld0"), sem("ld1")], [sem("xs0"), sem("xs1")]
        (qkT_done, qkT_ready, st_done, seg_done, dec_ready, d1_ready, M_ready, sr_done, Mr_ready, ssd_done, ret_done,
         weighed, xd_ready, new_states, state_ready, gates_ready, ms_ready, root_done, ycat_ready,
         yT_done, yT_ready, out_done, mixed, out_stored, chain, zeroed, mixchain) = (
            sem(n) for n in ("qkTd", "qkTr", "std", "seg", "dec", "d1", "M", "sr", "Mr", "ssd", "ret",
                             "weighed", "xd", "news", "state", "gates", "ms", "root", "ycat",
                             "yTd", "yTr", "outd", "mixed", "outst", "chain", "zeroed", "mixchain"))
        h8 = lambda ap: ap.rearrange("p (h d) -> p h d", h=HEADS)
        row8 = lambda tt, t, d: tt[:, bass.ds(t, 1), 8 * d:8 * d + 8].rearrange("p o h -> p (o h)")
        ctx.callback(clear_sems, nc, sems)
        block = ctx.enter_context(nc.Block())

        def steps(eng, body):
            body(0, 0, 0, 0)
            with eng.Fori(0, (NT - 1) // 2) as i:
                body(i * 2 + 1, 1, 1, i * 2 + 2)
                body(i * 2 + 2, 0, 1, i * 2 + 3)

        @block.sync
        def _(sp):
            for dst, src in ((skip[:], bcast_rows(g.skip_row)), (nw[:], bcast_rows(g.ssm_w)), (gw[:], bcast_rows(g.gn_w)),
                             (gb[:], bcast_rows(g.gn_b)), (g1[:, 0], bcast_rows(g.mod_d[0, 2 * D:3 * D])),
                             (g1[:, 1], bcast_rows(g.mod_d[1, 2 * D:3 * D])), (wo, g.w_out.rearrange("(k p) n -> p k n", p=P))):
                sp.dma_start(dst, src).then_inc(small, 16)
            sp.sem_inc(mixed, 2)
            sp.sem_inc(x_stored[0], 16)
            sp.sem_inc(x_stored[1], 16)

            def load(n, s, seq, b):
                sp.wait_ge(mixed, n + 1)
                sp.wait_ge(x_stored[s], (n // 2) * 16 + 16)
                rows = bass.ds(n * P, P)
                for dst, src in ((zvg[s][:, 0:W_], g.tok_d[rows, 0:W_]), (zvg[s][:, W_:], g.tok_d[rows, 3 * W_:5 * W_]),
                                 (bc[s][:], g.xbc_d[4 * P:, :].rearrange("(c p) t -> p c t", p=P)[:, :, rows]),
                                 (rec[s][:], g.rec_d[rows, :]), (xt[s][:], g.x_all[rows, :])):
                    sp.dma_start(dst, src).then_inc(loaded[s], 16)
                if isinstance(n, int):
                    sp.wait_ge(state_ready, 1)
                    sp.dma_start(g.ssd_f_out, sf[:]).then_inc(out_stored, 16)
                    sp.dma_start(g.ret_f_out.rearrange("n (h d) -> n h d", h=HEADS), sfr).then_inc(out_stored, 16)
                    sp.wait_ge(out_stored, 32)
                    sp.dma_start(sf[:], g.ssd_fwd_T).then_inc(out_stored, 16)
                    sp.dma_start(sfr, g.ret_fwd_T.rearrange("n (h d) -> n h d", h=HEADS)).then_inc(out_stored, 16)
            steps(sp, load)
            for s in range(2):
                sp.wait_ge(x_stored[s], 16 * (NT // 2 + 2 - s))

        @block.gpsimd
        def _(pool):
            pool.wait_ge(small, 7 * 16)

            def step(n, s, seq, b):
                pool.wait_ge(loaded[s], (n // 2) * 80 + 80)
                if not isinstance(n, int):
                    pool.wait_ge(new_states, n)
                x8 = h8(rec[s][:, 0:W_])
                pool.tensor_tensor(h8(xw[:]), x8, row8(g.WD, n, 0).unsqueeze(2).broadcast_to([P, HEADS, HD]), ALU.mult).then_inc(weighed, 1)
                pool.tensor_tensor(h8(vw[:]), h8(zvg[s][:, W_:2 * W_]), heads_bcast(g.WD[:, NT, 0:8]), ALU.mult).then_inc(weighed, 1)
                pool.tensor_copy(sr[:, :, 1, :], g.SBr[:, bass.ds(b, 1), :].rearrange("p o (h d) -> p (o h) d", h=HEADS)).then_inc(weighed, 1)
                pool.wait_ge(dec_ready, n * 4 + 4)
                pool.tensor_tensor(dec[:, 8:16, :], dec[:, 8:16, :],
                                   row8(g.DT, n, 1).unsqueeze(2).broadcast_to([P, HEADS, P]), ALU.mult).then_inc(d1_ready, 1)
                if not isinstance(n, int):
                    pool.wait_ge(ycat_ready, n)
                pool.tensor_tensor(y[:], rec[s][:, 0:W_], skip[:], ALU.mult).then_inc(xd_ready, 1)
            steps(pool, step)

        @block.scalar
        def _(act):
            def step(n, s, seq, b):
                act.wait_ge(loaded[s], (n // 2) * 80 + 80)
                act.wait_ge(qkT_done, n + 1)
                if not isinstance(n, int):
                    act.wait_ge(new_states, n)
                for q in range(4):
                    z = act.activation(qkT[:, 4 * q:4 * q + 4, :].rearrange("p h t -> p (h t)"), g.ps[q][0:HD, :], ACT.Copy)
                    z.then_inc(qkT_ready, 1)
                if not isinstance(n, int):
                    act.wait_ge(M_ready, n)
                for q in range(4):
                    act.wait_ge(seg_done, n * 4 + q + 1)
                    for h in range(4):
                        c = 4 * q + h
                        z = act.activation(dec[:, c, :], g.ps[(5, 6, 7, 0)[q]][:, h * P:(h + 1) * P], ACT.Exp,
                                           bias=g.NC[:, bass.ds(n, 1), c])
                    z.then_inc(dec_ready, 1)
                if not isinstance(n, int):
                    act.wait_ge(ycat_ready, n)
                act.activation(gate[:, 0, :], zvg[s][:, 0:W_], ACT.Silu)
                act.activation(gate[:, 1, :], zvg[s][:, 2 * W_:], ACT.Silu).then_inc(gates_ready, 1)
                if not isinstance(n, int):
                    turn(n - 1, 1 - s)
                act.wait_ge(ms_ready, n + 1)
                act.activation(st[:], st[:], ACT.Sqrt).then_inc(root_done, 1)

            def turn(n, s):
                act.wait_ge(yT_done, n + 1)
                for q in range(2):
                    z = act.activation(yT[:, 4 * q:4 * q + 4, :].rearrange("p k t -> p (k t)"), g.ps[(3, 5)[q]][:], ACT.Copy)
                z.then_inc(yT_ready, 1)
                act.wait_ge(mixed, n + 3)
                act.dma_start(g.x1_d[bass.ds(n * P, P), :], xt[s][:]).then_inc(x_stored[s], 16)
            steps(act, step)
            turn(NT - 1, 0)

        @block.vector
        def _(dve):
            own = Chain(dve, chain)
            own.link(dve.memset(sf[:], 0.0))
            own.link(dve.memset(sfr, 0.0))
            dve.sem_inc(zeroed, 1)
            dve.wait_ge(small, 7 * 16)
            PRE = own.n

            def link(ins):
                ins.then_inc(chain, 1)
                own.n += 1
                dve.wait_ge(chain, own.base + own.n + PRE)

            def step(n, s, seq, b):
                own.step(n)
                dve.wait_ge(loaded[s], (n // 2) * 80 + 80)
                dve.wait_ge(dec_ready, n * 4 + 2)
                link(dve.tensor_tensor(dec[:, 0:8, :], dec[:, 0:8, :], row8(g.DT, n, 0).unsqueeze(2).broadcast_to([P, HEADS, P]), ALU.mult))
                dve.wait_ge(d1_ready, n + 1)
                link(dve.tensor_tensor(dec[:, 0:8, :], dec[:, 0:8, :], dec[:, 8:16, :], ALU.add))
                dve.wait_ge(st_done, n + 1)
                for gr in range(2):
                    z = dve.tensor_tensor(M[:, 4 * gr:4 * gr + 4, :], dec[:, 4 * gr:4 * gr + 4, :],
                                          g.ps[4][:, gr * P:(gr + 1) * P].unsqueeze(1).broadcast_to([P, 4, P]), ALU.mult)
                    link(z)
                dve.sem_inc(M_ready, 1)
                dve.wait_ge(sr_done, n + 1)
                for q in range(2):
                    link(dve.tensor_tensor(Mr[:, 4 * q:4 * q + 4, :].rearrange("p h t -> p (h t)"),
                                           g.Dret[:, 4 * q:4 * q + 4, :].rearrange("p h t -> p (h t)"), g.ps[1 + q][:], ALU.mult))
                dve.sem_inc(Mr_ready, 1)
                if not isinstance(n, int):
                    mix(n - 1, 1 - s)
                dve.wait_ge(ssd_done, n + 1)
                dve.tensor_tensor(h8(t1[:]), h8(g.ps[3][:]), row8(g.EC, n, 0).unsqueeze(2).broadcast_to([P, HEADS, HD]), ALU.mult)
                link(dve.tensor_tensor(h8(t2[:]), h8(g.ps[5][:]), row8(g.EC, n, 1).unsqueeze(2).broadcast_to([P, HEADS, HD]), ALU.mult))
                link(dve.tensor_tensor(t1[:], t1[:], g.ps[6][:], ALU.add))
                dve.wait_ge(xd_ready, n + 1)
                link(dve.tensor_tensor(t2[:], t2[:], y[:], ALU.add))
                link(dve.tensor_tensor(y[:], t1[:], t2[:], ALU.add))
                dve.wait_ge(gates_ready, n + 1)
                link(dve.tensor_tensor(y[:], y[:], gate[:, 0, :], ALU.mult))
                link(dve.tensor_tensor_reduce(t1[:], y[:], y[:], 1.0 / W_, EPS, ALU.mult, ALU.add, st[:, 0:1]))
                dve.wait_ge(ret_done, n + 1)
                for d, rr in enumerate((r, r2)):
                    for q, bank in enumerate((7, 0)):
                        z = dve.tensor_tensor(h8(rr[:])[:, 4 * q:4 * q + 4, :], g.ps[bank][:].rearrange("p (h f d) -> p h f d", f=2, d=HD)[:, :, d, :],
                                              heads_bcast(g.EC[:, NT, 8 * d:8 * d + 8])[:, 4 * q:4 * q + 4, :], ALU.mult)
                        z.then_inc(chain, 1)
                        own.n += 1
                dve.wait_ge(chain, own.base + own.n + PRE)
                link(dve.tensor_tensor(r[:], r[:], g.ps[4][:], ALU.add))
                link(dve.tensor_tensor(r[:], r[:], r2[:], ALU.add))
                link(dve.tensor_reduce(mean[:], h8(r[:]), AXX, ALU.add))
                link(dve.tensor_scalar(mean[:], mean[:], 1.0 / HD, None, ALU.mult))
                link(dve.tensor_tensor(h8(r[:]), h8(r[:]), heads_bcast(mean[:]), ALU.subtract))
                link(dve.tensor_tensor(r2[:], r[:], r[:], ALU.mult))
                link(dve.tensor_reduce(st[:, 1:9], h8(r2[:]), AXX, ALU.add))
                link(dve.tensor_scalar(st[:, 1:9], st[:, 1:9], 1.0 / HD, EPS, ALU.mult, ALU.add))
                dve.sem_inc(ms_ready, 1)
                dve.wait_ge(new_states, n + 1)
                if not isinstance(n, int):
                    dve.wait_ge(out_stored, 64)
                dve.tensor_tensor(h8(sf[:]), h8(sf[:]), row8(g.CD, n, 0).unsqueeze(2).broadcast_to([P, HEADS, HD]), ALU.mult)
                link(dve.tensor_tensor(sfr, sfr, heads_bcast(g.CD[0:HD, NT, 0:8]), ALU.mult))
                dve.tensor_tensor(sf[:], sf[:], g.ps[1][:], ALU.add)
                link(dve.tensor_tensor(sfr, sfr, h8(g.ps[2][0:HD, :]), ALU.add))
                dve.sem_inc(state_ready, 1)
                dve.wait_ge(root_done, n + 1)
                link(dve.reciprocal(st[:], st[:]))
                dve.scalar_tensor_tensor(ycat[:, 0:W_], y[:], st[:, 0:1], nw[:], ALU.mult, ALU.mult)
                link(dve.tensor_tensor(h8(r[:]), h8(r[:]), heads_bcast(st[:, 1:9]), ALU.mult))
                link(dve.tensor_tensor(r[:], r[:], gw[:], ALU.mult))
                link(dve.tensor_tensor(r[:], r[:], gb[:], ALU.add))
                link(dve.tensor_tensor(ycat[:, W_:], r[:], gate[:, 1, :], ALU.mult))
                dve.sem_inc(ycat_ready, 1)

            def mix(n, s):
                dve.wait_ge(out_done, n + 1)
                gain = lambda q: g1[:, bass.ds((n + 7) // 8, 1), q * 512:(q + 1) * 512].rearrange("p o (k c) -> p (o k) c", c=P)
                for q in range(2):
                    dve.tensor_tensor(gained[:, 4 * q:4 * q + 4, :], g.ps[6 + q][:].rearrange("p (k c) -> p k c", c=P), gain(q), ALU.mult).then_inc(mixchain, 1)
                dve.wait_ge(mixchain, n * 3 + 2)
                dve.tensor_tensor(xt[s][:].rearrange("p (k c) -> p k c", c=P), xt[s][:].rearrange("p (k c) -> p k c", c=P), gained, ALU.add).then_inc(mixchain, 1)
                dve.wait_ge(mixchain, n * 3 + 3)
                dve.sem_inc(mixed, 1)
            steps(dve, step)
            mix(NT - 1, 0)

        @block.tensor
        def _(pe):
            pe.wait_ge(small, 7 * 16)

            def step(n, s, seq, b):
                first = isinstance(n, int)
                pe.wait_ge(loaded[s], (n // 2) * 80 + 80)
                if not first:
                    pe.wait_ge(state_ready, n)
                qk = W_ + 2 * P
                for gr in range(2):
                    mm = pe.matmul(g.ps[4][:, gr * P:(gr + 1) * P], bc[s][:, gr, :], bc[s][:, 2 + gr, :], start=True, stop=True)
                mm.then_inc(st_done, 1)
                for c in range(16):
                    mm = pe.transpose(g.ps[c // 4][0:HD, (c % 4) * P:(c % 4 + 1) * P], rec[s][:, qk + c * HD:qk + (c + 1) * HD], g.ident[:])
                mm.then_inc(qkT_done, 1)
                for q in range(4):
                    if q == 3:
                        pe.wait_ge(qkT_ready, n * 4 + 4)
                    segment(pe, g, q, g.ps[(5, 6, 7, 0)[q]], n).then_inc(seg_done, 1)
                for h in range(HEADS):
                    mm = pe.matmul(g.ps[1 + h // 4][:, (h % 4) * P:(h % 4 + 1) * P], qkT[:, 8 + h, :], qkT[:, h, :], start=True, stop=True)
                mm.then_inc(sr_done, 1)
                pe.wait_ge(dec_ready, n * 4 + 1)
                if not first:
                    project(n - 1)
                if not first:
                    pe.wait_ge(out_stored, 64)
                pe.wait_ge(zeroed, 1)
                for gr in range(2):
                    c = bc[s][:, 2 + gr, :]
                    cols = slice(gr * 256, (gr + 1) * 256)
                    pe.matmul(g.ps[3][:, cols], c, sf[:, cols], start=True, stop=True)
                    pe.matmul(g.ps[5][:, cols], c, g.SB[:, bass.ds(b, 1), cols].rearrange("p o c -> p (o c)"), start=True, stop=True)
                pe.wait_ge(M_ready, n + 1)
                if not first:
                    pe.wait_ge(mixed, n + 2)
                for h in range(HEADS):
                    cols = slice(h * HD, (h + 1) * HD)
                    mm = pe.matmul(g.ps[6][:, cols], M[:, h, :], rec[s][:, cols], start=True, stop=True)
                mm.then_inc(ssd_done, 1)
                pe.wait_ge(weighed, n * 3 + 3)
                for h in range(HEADS):
                    pe.matmul(g.ps[(7, 0)[h // 4]][:, (h % 4) * P:(h % 4 + 1) * P], qkT[:, h, :],
                              sr[:, h].rearrange("p f d -> p (f d)"), start=True, stop=True)
                pe.wait_ge(Mr_ready, n + 1)
                for h in range(HEADS):
                    cols = slice(h * HD, (h + 1) * HD)
                    mm = pe.matmul(g.ps[4][:, cols], Mr[:, h, :], zvg[s][:, W_ + h * HD:W_ + (h + 1) * HD], start=True, stop=True)
                mm.then_inc(ret_done, 1)
                for gr in range(2):
                    cols = slice(gr * 256, (gr + 1) * 256)
                    pe.matmul(g.ps[1][:, cols], rec[s][:, W_ + gr * P:W_ + (gr + 1) * P], xw[:, cols], start=True, stop=True)
                for h in range(HEADS):
                    cols = slice(h * HD, (h + 1) * HD)
                    k = rec[s][:, qk + W_ + h * HD:qk + W_ + (h + 1) * HD]
                    mm = pe.matmul(g.ps[2][0:HD, cols], k, vw[:, cols], start=True, stop=True)
                mm.then_inc(new_states, 1)

            def project(n):
                pe.wait_ge(ycat_ready, n + 1)
                for k in range(KD):
                    mm = pe.transpose(g.ps[(3, 5)[k // 4]][:, (k % 4) * P:(k % 4 + 1) * P], ycat[:, k * P:(k + 1) * P], g.ident[:])
                mm.then_inc(yT_done, 1)
                pe.wait_ge(yT_ready, n + 1)
                for q in range(2):
                    for k in range(KD):
                        mm = pe.matmul(g.ps[6 + q][:], yT[:, k, :], wo[:, k, q * 512:(q + 1) * 512], start=(k == 0), stop=(k == KD - 1))
                mm.then_inc(out_done, 1)
            steps(pe, step)
            project(NT - 1)


def select_experts(nc, g):
    NH, Q = 2 * HEADS, 4
    with ExitStack() as ctx:
        sb = lambda n, s, d=F32: ctx.enter_context(nc.sbuf_tensor(n, s, d))
        sems = []
        sem = lambda n: new_sem(nc, ctx, f"tk_{n}", sems)
        sc = [sb(f"tksc{i}", [P, NH, NKEY]) for i in range(2)]
        best, place = sb("best", [P, NH, TOPK]), sb("place", [P, NH, TOPK], U32)
        placef = sb("placef", [P, HEADS, 2, TOPK])
        cand = sb("cand", [P, HEADS, TOPK, TOPK])
        top, pos = sb("top", [P, HEADS, TOPK]), sb("pos", [P, HEADS, TOPK], U32)
        ab, abf = sb("ab", [P, 2, NSEL], U32), sb("abf", [P, 2, NSEL])
        hit = [sb(f"hit{i}", [P, NSEL, TOPK]) for i in range(2)]
        out3 = sb("out3", [P, 3, NSEL])
        den = sb("den", [P, HEADS])
        iota16 = sb("iota16", [P, TOPK])
        small, copied, top_ready, exp_ready, ab_ready, hit_ready, out_ready, turned, done, chain, pchain = (
            sem(n) for n in ("small", "copied", "top", "exp", "ab", "hit", "out", "turned", "done", "chain", "pchain"))
        searched, fchain = sem("searched"), sem("fchain")
        pad, ppad = sb("tkpad", [P, 1]), sb("tkppad", [P, 1])
        qT, keys = sb("qT", [P, 2, 4, P]), sb("keys", [P, NH, NKEY])
        keys_in, hT_stored, q_done, qT_ready, s_done = (sem(n) for n in ("keys", "hst", "q", "qT", "s"))
        i16 = iota16[:].unsqueeze(1).broadcast_to([P, NSEL, TOPK])
        ctx.callback(clear_sems, nc, sems)
        block = ctx.enter_context(nc.Block())

        def tiles(eng, body, ahead=None):
            if ahead is None:
                body(0, 0)
                with eng.Fori(0, (NT - 1) // 2) as i:
                    body(i * 2 + 1, 1)
                    body(i * 2 + 2, 0)
                return
            ahead(0, 0)
            ahead(1, 1)
            ahead(2, 0)
            body(0, 0)
            with eng.Fori(0, (NT - 3) // 2) as i:
                ahead(i * 2 + 3, 1)
                body(i * 2 + 1, 1)
                ahead(i * 2 + 4, 0)
                body(i * 2 + 2, 0)
            body(NT - 2, 1)
            body(NT - 1, 0)

        def spread(p):
            return placef[:, :, p, :].unsqueeze(2).broadcast_to([P, HEADS, TOPK, TOPK])

        @block.sync
        def _(sp):
            sp.dma_start(iota16[:], g.iota_d[:, 0:TOPK]).then_inc(small, 16)
            sp.dma_start(keys[:], g.keys_T).then_inc(keys_in, 16)
            sp.dma_start(g.h2T_d, g.hT[:]).then_inc(hT_stored, 16)
            sp.wait_ge(hT_stored, 16)

        @block.scalar
        def _(act):
            act.sem_inc(done, 1)
            act.sem_inc(qT_ready, 2)
            act.sem_inc(copied, 2)

            def evacuate(n, s):
                def query(j):
                    act.wait_ge(q_done, n * Q + j + 1)
                    act.activation(qT[:, j % 2].rearrange("p h t -> p (h t)"), g.ps[1 + j % 2][:], ACT.Copy).then_inc(qT_ready, 1)

                def score(j):
                    act.wait_ge(s_done, n * Q + j + 1)
                    if j == 0 and not (isinstance(n, int) and n < 2):
                        act.wait_ge(searched, n - 1)
                    act.activation(sc[s][:, 4 * j:4 * j + 4, :].rearrange("p h c -> p (h c)"), g.ps[3 + j % 2][:], ACT.Copy).then_inc(copied, 1)
                query(0)
                for j in range(1, Q):
                    query(j)
                    score(j - 1)
                score(Q - 1)

            def tile(n, s):
                act.wait_ge(top_ready, n + 1)
                act.activation(out3[:, 2], out3[:, 2], ACT.Exp).then_inc(exp_ready, 1)
                act.wait_ge(turned, n + 1)
                act.activation(g.sel3[:, :, bass.ds(n * P, P)], g.ps[0][:, 0:3 * P].rearrange("p (c t) -> p c t", c=3), ACT.Copy).then_inc(done, 1)
            tiles(act, tile, evacuate)

        @block.gpsimd
        def _(pool):
            pool.wait_ge(small, 16)

            def tile(n, s):
                pool.wait_ge(ab_ready, n + 1)
                if not isinstance(n, int):
                    pool.wait_ge(out_ready, n)
                pool.tensor_tensor(hit[0][:], abf[:, 0].unsqueeze(2).broadcast_to([P, NSEL, TOPK]), i16, ALU.subtract).then_inc(pchain, 1)
                pool.wait_ge(pchain, n * 3 + 1)
                pool.tensor_tensor(ppad[:], iota16[:, 0:1], iota16[:, 0:1], ALU.add)
                pool.tensor_scalar(hit[0][:], hit[0][:], 0.0, None, ALU.is_equal).then_inc(pchain, 1)
                pool.wait_ge(pchain, n * 3 + 2)
                h4 = hit[0][:].rearrange("p (h k) a -> p h k a", h=HEADS)
                pool.tensor_tensor(h4, h4, spread(0), ALU.mult).then_inc(pchain, 1)
                pool.wait_ge(pchain, n * 3 + 3)
                pool.sem_inc(hit_ready, 1)
            tiles(pool, tile)

        @block.vector
        def _(dve):
            own = Chain(dve, chain)
            link = own.link
            dve.wait_ge(small, 16)

            def tile(n, s):
                own.step(n)
                dve.wait_ge(copied, n * Q + (Q + 2))
                def rounds(values, best_of, place_of, lists):
                    for r in range(2):
                        dve.memset(pad[:], 0.0)
                        for i in range(lists):
                            z = dve.max(best_of(i)[:, 8 * r:8 * r + 8], values(i))
                        link(z)
                        dve.memset(pad[:], 0.0)
                        for i in range(lists):
                            z = dve.max_index(place_of(i)[:, 8 * r:8 * r + 8], best_of(i)[:, 8 * r:8 * r + 8], values(i))
                        link(z)
                        if r == 0:
                            dve.memset(pad[:], 0.0)
                            for i in range(lists):
                                z = dve.match_replace(values(i), best_of(i)[:, 0:8], values(i), LOW)
                            link(z)
                rounds(lambda i: sc[s][:, i, :], lambda i: best[:, i, :], lambda i: place[:, i, :], NH)
                dve.sem_inc(searched, 1)
                if not isinstance(n, int):
                    finish(n - 1)
                dve.tensor_copy(placef[:].rearrange("p h s k -> p (h s) k"), place[:])
                b4 = best[:].rearrange("p (h s) k -> p h s k", s=2)
                link(dve.tensor_tensor(cand[:], b4[:, :, 0, :].unsqueeze(3).broadcast_to([P, HEADS, TOPK, TOPK]),
                                       b4[:, :, 1, :].unsqueeze(2).broadcast_to([P, HEADS, TOPK, TOPK]), ALU.add))
                rounds(lambda i: cand[:, i].rearrange("p a b -> p (a b)"), lambda i: top[:, i, :], lambda i: pos[:, i, :], HEADS)
                if not isinstance(n, int):
                    dve.wait_ge(turned, n)
                o = out3[:, 2].rearrange("p (h k) -> p h k", h=HEADS)
                link(dve.tensor_tensor(o, top[:], top[:, :, 0:1].broadcast_to([P, HEADS, TOPK]), ALU.subtract))
                dve.sem_inc(top_ready, 1)
                p1 = pos[:].rearrange("p h k -> p (h k)")
                dve.tensor_scalar(ab[:, 0], p1, 4, None, ALU.logical_shift_right)
                link(dve.tensor_scalar(ab[:, 1], p1, 15, None, ALU.bitwise_and))
                link(dve.tensor_copy(abf[:], ab[:]))
                dve.sem_inc(ab_ready, 1)
                link(dve.tensor_tensor(hit[1][:], abf[:, 1].unsqueeze(2).broadcast_to([P, NSEL, TOPK]), i16, ALU.is_equal))
                h4 = hit[1][:].rearrange("p (h k) a -> p h k a", h=HEADS)
                link(dve.tensor_tensor(h4, h4, spread(1), ALU.mult))
                link(dve.tensor_reduce(out3[:, 1], hit[1][:], AXX, ALU.add))

            def finish(n):
                def fix(ins, i):
                    ins.then_inc(fchain, 1)
                    dve.wait_ge(fchain, n * 4 + i)
                o = out3[:, 2].rearrange("p (h k) -> p h k", h=HEADS)
                dve.wait_ge(exp_ready, n + 1)
                fix(dve.tensor_reduce(den[:], o, AXX, ALU.add), 1)
                fix(dve.reciprocal(den[:], den[:]), 2)
                fix(dve.tensor_tensor(o, o, den[:].unsqueeze(2).broadcast_to([P, HEADS, TOPK]), ALU.mult), 3)
                dve.wait_ge(hit_ready, n + 1)
                fix(dve.tensor_reduce(out3[:, 0], hit[0][:], AXX, ALU.add), 4)
                dve.sem_inc(out_ready, 1)
            tiles(dve, tile)
            finish(NT - 1)

        @block.tensor
        def _(pe):
            pe.wait_ge(keys_in, 16)

            def scores(n, s):
                def query(j):
                    pe.wait_ge(qT_ready, n * Q + j + 1)
                    for h in range(4):
                        for k in range(KD):
                            mm = pe.matmul(g.ps[1 + j % 2][:, h * P:(h + 1) * P], g.wq[:, k, (4 * j + h) * P:(4 * j + h + 1) * P],
                                           g.hT[:, k, bass.ds(n * P, P)], start=(k == 0), stop=(k == KD - 1))
                    mm.then_inc(q_done, 1)

                def score(j):
                    pe.wait_ge(qT_ready, n * Q + j + 3)
                    pe.wait_ge(copied, n * Q + j + 1)
                    for h in range(4):
                        mm = pe.matmul(g.ps[3 + j % 2][:, h * P:(h + 1) * P], qT[:, j % 2, h, :], keys[:, 4 * j + h, :], start=True, stop=True)
                    mm.then_inc(s_done, 1)
                query(0)
                for j in range(1, Q):
                    query(j)
                    score(j - 1)
                score(Q - 1)

            def tile(n, s):
                pe.wait_ge(out_ready, n + 1)
                pe.wait_ge(done, n + 1)
                for c in range(3):
                    mm = pe.transpose(g.ps[0][:, c * P:(c + 1) * P], out3[:, c], g.ident[:])
                mm.then_inc(turned, 1)
            tiles(pe, tile, scores)


def gather_inputs(nc, g):
    with ExitStack() as ctx:
        sb = lambda n, s, d=F32: ctx.enter_context(nc.sbuf_tensor(n, s, d))
        sems = []
        sem = lambda n: new_sem(nc, ctx, f"gi_{n}", sems)
        rows, pick = sb("gih", [P, GT, D]), sb("gipick", [P, 2, GT, NSEL])
        first = sb("gifirst", [P, GT, NSEL])
        turned, copied, numbered, stored, chain = (sem(n) for n in ("turned", "copied", "numbered", "stored", "chain"))
        ctx.callback(clear_sems, nc, sems)
        block = ctx.enter_context(nc.Block())

        @block.tensor
        def _(pe):
            for q in range(GT):
                for k in range(KD):
                    mm = pe.transpose(g.ps[2 * q + k // 4][:, (k % 4) * P:(k % 4 + 1) * P], g.hT[:, k, q * P:(q + 1) * P], g.ident[:])
                for c in range(3):
                    mm = pe.transpose(g.ps[6 + q][:, c * P:(c + 1) * P], g.sel3[:, c, q * P:(q + 1) * P], g.ident[:])
                mm.then_inc(turned, 1)

        @block.scalar
        def _(act):
            for q in range(GT):
                act.wait_ge(turned, q + 1)
                for j in range(2):
                    z = act.activation(rows[:, q, j * 512:(j + 1) * 512], g.ps[2 * q + j][:], ACT.Copy)
            z.then_inc(copied, 1)

        @block.vector
        def _(dve):
            for q in range(GT):
                dve.wait_ge(turned, q + 1)
                dve.tensor_scalar(first[:, q], g.ps[6 + q][:, 0:P], float(NKEY), None, ALU.mult).then_inc(chain, 1)
                dve.wait_ge(chain, q + 1)
                dve.tensor_tensor(pick[:, 0, q], first[:, q], g.ps[6 + q][:, P:2 * P], ALU.add)
                z = dve.tensor_copy(pick[:, 1, q], g.ps[6 + q][:, 2 * P:3 * P])
            z.then_inc(numbered, 1)

        @block.sync
        def _(sp):
            sp.wait_ge(copied, 1)
            sp.dma_start(g.rows_d, rows[:]).then_inc(stored, 16)
            sp.wait_ge(numbered, 1)
            sp.dma_start(g.pick_d, pick[:]).then_inc(stored, 16)
            sp.wait_ge(stored, 32)


def dense_gates(nc, g):
    G, B, R = 8, 2, 4
    RT = P // G
    with ExitStack() as ctx:
        sb = lambda n, s, d=F32: ctx.enter_context(nc.sbuf_tensor(n, s, d))
        sems = []
        sem = lambda n: new_sem(nc, ctx, f"dg_{n}", sems)
        one, two = ([g.hT[:, i * R + s, 0:G * P].rearrange("p (g c) -> p g c", c=P) for s in range(R)] for i in range(2))
        iota = sb("iota", [P, P])
        out = [sb(f"gates{i}", [P, NKEY, P]) for i in range(2)]
        small, one_ready, two_ready, gated, prod, copied, stored = (
            sem(n) for n in ("small", "one", "two", "gated", "prod", "copied", "stored"))
        stored = [stored, sem("stored1")]
        ctx.callback(clear_sems, nc, sems)
        block = ctx.enter_context(nc.Block())

        def tiles(eng, body):
            body(0, 0)
            with eng.Fori(0, (DENSE - 1) // 2) as i:
                body(i * 2 + 1, 1)
                body(i * 2 + 2, 0)

        def of_tokens(c, t):
            return g.sel3[:, c, bass.ds(t + GT * P, G)].unsqueeze(2).broadcast_to([P, G, P])

        @block.sync
        def _(sp):
            sp.dma_start(iota[:], g.iota_d).then_inc(small, 16)
            sp.sem_inc(stored[0], 16)
            sp.sem_inc(stored[1], 16)
            sp.sem_inc(prod, R * B)

            def store(t, s):
                sp.wait_ge(copied, t * (RT * B) + (RT * B + 2 * B))
                sp.dma_start(g.gates_d.rearrange("b a t -> a b t")[:, :, bass.ds(t * P, P)], out[s][:]).then_inc(stored[s], 16)
            tiles(sp, store)
            sp.wait_ge(stored[0], 16 * ((DENSE + 1) // 2 + 1))
            sp.wait_ge(stored[1], 16 * (DENSE // 2 + 1))

        @block.vector
        def _(dve):
            dve.wait_ge(small, 16)
            numbers = iota[:].unsqueeze(1).broadcast_to([P, G, P])
            with dve.Fori(0, TE // (R * G)) as i:
                for s in range(R):
                    dve.wait_ge(prod, i * (R * B) + (s + 1) * B)
                    dve.tensor_tensor(one[s], numbers, of_tokens(0, i * (R * G) + s * G), ALU.is_equal).then_inc(one_ready, 1)
                    dve.tensor_tensor(two[s], numbers, of_tokens(1, i * (R * G) + s * G), ALU.is_equal).then_inc(two_ready, 1)

        @block.gpsimd
        def _(pool):
            with pool.Fori(0, TE // (R * G)) as i:
                for s in range(R):
                    pool.wait_ge(one_ready, i * R + s + 1)
                    pool.tensor_tensor(one[s], one[s], of_tokens(2, i * (R * G) + s * G), ALU.mult).then_inc(gated, 1)

        @block.tensor
        def _(pe):
            with pe.Fori(0, TE // (R * G)) as i:
                for s in range(R):
                    r = i * R + s
                    pe.wait_ge(two_ready, r + 1)
                    pe.wait_ge(gated, r + 1)
                    for b in range(B):
                        pe.wait_ge(copied, r * B + b + 1)
                        for j in range(G // B):
                            q = b * (G // B) + j
                            mm = pe.matmul(g.ps[2 * (s % 2) + b][:, j * P:(j + 1) * P], one[s][:, q], two[s][:, q], start=True, stop=True)
                        mm.then_inc(prod, 1)

        @block.scalar
        def _(act):
            act.sem_inc(copied, 2 * B)

            def tile(t, s):
                act.wait_ge(stored[s], (t // 2) * 16 + 16)
                with act.Fori(0, RT // 2) as i:
                    for h in range(2):
                        for b in range(B):
                            act.wait_ge(prod, t * (RT * B) + i * (2 * B) + (h * B + b + 1 + R * B))
                            first = i * (2 * G) + (h * G + b * (G // B))
                            act.activation(out[s][:, :, bass.ds(first, G // B)].rearrange("p c t -> p t c"),
                                           g.ps[2 * h + b][:].rearrange("p (t c) -> p t c", c=P), ACT.Copy).then_inc(copied, 1)
            tiles(act, tile)


def experts(nc, g):
    TG, NE = TE // 2, NKEY
    NB = TE // TG
    SL = NSEL // (NE // 2)
    with ExitStack() as ctx:
        sb = lambda n, s, d=F32: ctx.enter_context(nc.sbuf_tensor(n, s, d))
        sems = []
        sem = lambda n: new_sem(nc, ctx, f"ex_{n}", sems)
        pair = lambda n, s, d=F32: [sb(f"{n}{i}", s, d) for i in range(2)]
        h_hi, h_lo = sb("h_hi", [P, KD, TE], F32R), sb("h_lo", [P, KD, TE], F32R)
        uw, u_hi, u_lo = pair("uw", [P, KD, P]), pair("u_hi", [P, KD, P], F32R), pair("u_lo", [P, KD, P], F32R)
        vw, v_hi, v_lo = pair("vw", [P, D]), pair("v_hi", [P, D], F32R), pair("v_lo", [P, D], F32R)
        gt, a, a_hi, a_lo = pair("gt", [P, TE]), pair("ga", [P, TE]), pair("a_hi", [P, TE], F32R), pair("a_lo", [P, TE], F32R)
        f = lambda ap: ap.bitcast(F32)
        psem = lambda n: [sem(n + "0"), sem(n + "1")]
        h_loaded, u_loaded, v_loaded, g_loaded = psem("h"), psem("ul"), psem("vl"), psem("gl")
        (h_hi_ready, h_lo_ready, u_hi_ready, u_lo_ready, v_hi_ready, v_lo_ready, s_done, act_done, a_ready, a_hi_ready,
         a_lo_ready, y_done, y_added, zeroed) = (
            sem(n) for n in ("hhi", "hlo", "uhi", "ulo", "vhi", "vlo", "s", "act", "a", "ahi", "alo", "y", "yadd", "z"))
        hrow, pick = sb("hrow", [P, GT, D]), sb("pick", [P, 2, GT, NSEL])
        uu, vv = pair("urows", [P, D]), pair("vrows", [P, D])
        at, dots, coef = pair("at", [P, SL], U32), pair("dots", [P, SL]), sb("coef", [P, SL])
        (picks, u_rows, v_rows, at_ready, dots_ready, gelu_ready, rchain) = (
            sem(n) for n in ("picks", "urows", "vrows", "at", "dots", "gelu", "rchain"))
        ppad = sb("gpad", [P, 2])
        ctx.callback(clear_sems, nc, sems)
        block = ctx.enter_context(nc.Block())
        YP, YB = 2 * (NT - GT), 4
        bank = lambda m: 4 + m % YB

        def load_u(sp, e, s):
            sp.dma_start(uw[s][:], g.u_T[bass.ds(e, 1)].rearrange("o p k c -> p (o k) c")).then_inc(u_loaded[s], 16)

        def load_v(sp, e, s):
            sp.dma_start(vw[s][:], g.peer_v[:, bass.ds(e, 1), :].rearrange("p o d -> p (o d)")).then_inc(v_loaded[s], 16)

        def load_g(sp, e, s):
            sp.dma_start(gt[s][:], g.gates_d[bass.ds(e, 1)].rearrange("o p t -> p (o t)")).then_inc(g_loaded[s], 16)

        @block.sync
        def _(sp):
            sp.dma_start(hrow[:], g.rows_d).then_inc(picks, 16)
            sp.dma_start(pick[:], g.pick_d).then_inc(picks, 16)
            for k in range(KD):
                s = k % 2
                if k >= 2:
                    sp.wait_ge(h_lo_ready, k - 1)
                sp.dma_start(gt[s][:], g.h2T_d[:, k, GT * P:T]).then_inc(h_loaded[s], 16)
                if k < 2:
                    load_u(sp, k, k)
                    load_v(sp, k, k)
            for s in range(2):
                sp.wait_ge(h_lo_ready, KD - 1 + s)
                load_g(sp, s, s)
            with sp.Fori(1, NE // 2) as j:
                for s in range(2):
                    e = j * 2 + s
                    sp.wait_ge(u_lo_ready, e - 1)
                    sp.wait_ge(u_hi_ready, e - 1)
                    load_u(sp, e, s)
                    sp.wait_ge(a_ready, e - 1)
                    load_g(sp, e, s)
                    sp.wait_ge(v_lo_ready, e - 1)
                    sp.wait_ge(v_hi_ready, e - 1)
                    load_v(sp, e, s)

        def split_u(act, e, s, j):
            act.wait_ge(u_loaded[s], j * 16 + 16)
            act.activation(u_hi[s][:], uw[s][:], ACT.Copy).then_inc(u_hi_ready, 1)

        @block.scalar
        def _(act):
            for k in range(KD):
                s = k % 2
                act.wait_ge(h_loaded[s], 16 * (k // 2 + 1))
                act.activation(h_hi[:, k, :], gt[s][:], ACT.Copy).then_inc(h_hi_ready, 1)
            split_u(act, 0, 0, 0)
            split_u(act, 1, 1, 0)

            def gelu_rows(p, q):
                act.wait_ge(dots_ready, p)
                act.activation(dots[q][:], dots[q][:], ACT.Gelu_apprx_tanh).then_inc(gelu_ready, 1)

            def block_(j, s, last=False):
                e = j * 2 + s
                act.wait_ge(s_done, e + 1)
                if not isinstance(j, int):
                    act.wait_ge(a_lo_ready, e - 1)
                for b in range(NB):
                    z = act.activation(a[s][:, b * TG:(b + 1) * TG], g.ps[2 * s + b][:, 0:TG], ACT.Gelu_apprx_tanh)
                z.then_inc(act_done, 1)
                if not last:
                    split_u(act, e + 2, s, j + 1)
                if s == 1 or not isinstance(j, int) or j > 0:
                    gelu_rows(j * GT + s, 1 - s)
                if not isinstance(j, int) or j > 0:
                    if s == 0:
                        act.wait_ge(y_done, j * YP)
                act.wait_ge(v_loaded[s], j * 16 + 16)
                act.activation(v_hi[s][:], vw[s][:], ACT.Copy).then_inc(v_hi_ready, 1)
                act.wait_ge(a_ready, e + 1)
                act.activation(a_hi[s][:], a[s][:], ACT.Copy).then_inc(a_hi_ready, 1)
            block_(0, 0)
            block_(0, 1)
            with act.Fori(1, NE // 2 - 1) as j:
                block_(j, 0)
                block_(j, 1)
            block_(NE // 2 - 1, 0, True)
            block_(NE // 2 - 1, 1, True)
            gelu_rows(NE // 2 * GT, 1)

        @block.gpsimd
        def _(pool):
            def low_u(s, e, j):
                pool.wait_ge(u_hi_ready, e + 1)
                pool.tensor_tensor(u_lo[s][:], uw[s][:], f(u_hi[s][:]), ALU.subtract).then_inc(u_lo_ready, 1)
            low_u(0, 0, 0)
            low_u(1, 1, 0)

            def gather(j, q, first=False, last=False):
                p = j * GT + q
                if not first:
                    pool.wait_ge(dots_ready, p)
                if not last:
                    pool.tensor_tensor(ppad[:, 0:1], g.ident[:, 0:1], g.ident[:, 0:1], ALU.add)
                    pool.tensor_copy(at[q][:], pick[:, 0, q, bass.ds(j * SL, SL)]).then_inc(at_ready, 1)
                    pool.wait_ge(at_ready, p + 1)
                    pool.tensor_tensor(ppad[:, 1:2], g.ident[:, 0:1], g.ident[:, 0:1], ALU.add)
                    for i in range(SL):
                        pool.indirect_dma_start(uu[i][:], None, g.u_rows, bass.IndirectOffsetOnAxis(ap=at[q][:, i:i + 1], axis=0)).then_inc(u_rows, 16)
                if not first:
                    for i in range(SL):
                        pool.indirect_dma_start(vv[i][:], None, g.v_rows, bass.IndirectOffsetOnAxis(ap=at[1 - q][:, i:i + 1], axis=0)).then_inc(v_rows, 16)
            pool.wait_ge(picks, 32)
            gather(0, 0, True)

            def low_v(j, s):
                pool.wait_ge(v_hi_ready, j * 2 + s + 1)
                pool.tensor_tensor(v_lo[s][:], vw[s][:], f(v_hi[s][:]), ALU.subtract).then_inc(v_lo_ready, 1)

            def pair_(j, last=False):
                if not last:
                    low_u(0, j * 2 + 2, j + 1)
                if not isinstance(j, int) or j > 0:
                    gather(j, 0)
                low_v(j, 0)
                gather(j, 1)
                if not last:
                    low_u(1, j * 2 + 3, j + 1)
                low_v(j, 1)
            pair_(0)
            with pool.Fori(1, NE // 2 - 1) as j:
                pair_(j)
            pair_(NE // 2 - 1, last=True)
            gather(NE // 2, 0, last=True)

        @block.vector
        def _(dve):
            dve.memset(g.Y[:], 0.0).then_inc(zeroed, 1)
            for k in range(KD):
                dve.wait_ge(h_hi_ready, k + 1)
                dve.tensor_tensor(h_lo[:, k, :], gt[k % 2][:], f(h_hi[:, k, :]), ALU.subtract).then_inc(h_lo_ready, 1)
            dve.sem_inc(y_added, YP)
            dve.wait_ge(picks, 32)
            dve.wait_ge(zeroed, 1)

            def gate(j, s):
                e = j * 2 + s
                dve.wait_ge(act_done, e + 1)
                dve.wait_ge(g_loaded[s], j * 16 + 16)
                dve.tensor_tensor(a[s][:], a[s][:], gt[s][:], ALU.mult).then_inc(a_ready, 1)

            def low(j, s):
                dve.wait_ge(a_hi_ready, j * 2 + s + 1)
                dve.tensor_tensor(a_lo[s][:], a[s][:], f(a_hi[s][:]), ALU.subtract).then_inc(a_lo_ready, 1)

            def add(j):
                for m in range(YP):
                    dve.wait_ge(y_done, j * YP + m + 1)
                    y = g.Y[:, GT + m // 2, (m % 2) * 512:(m % 2 + 1) * 512]
                    dve.tensor_tensor(y, y, g.ps[bank(m)][:], ALU.add).then_inc(y_added, 1)
                    if m == 1:
                        rows_v(j, 1)
                    if m == 5:
                        rows_u(j, 1)

            def rows_v(j, q):
                p = j * GT + q
                before, j0 = 1 - q, (j if q == 1 else j - 1)
                dve.wait_ge(gelu_ready, p)
                dve.tensor_tensor(coef[:], dots[before][:], pick[:, 1, before, bass.ds(j0 * SL, SL)], ALU.mult).then_inc(rchain, 1)
                dve.wait_ge(v_rows, p * (16 * SL))
                y = g.Y[:, before, :]
                for i in range(SL):
                    dve.wait_ge(rchain, p * (SL + 1) - (SL - i))
                    dve.scalar_tensor_tensor(y, vv[i][:], coef[:, i:i + 1], y, ALU.mult, ALU.add).then_inc(rchain, 1)

            def rows_u(j, q, first=False):
                p = j * GT + q
                if not first:
                    dve.wait_ge(rchain, p * (SL + 1))
                dve.wait_ge(u_rows, p * (16 * SL) + 16 * SL)
                for i in range(SL):
                    z = dve.tensor_tensor_reduce(uu[i][:], uu[i][:], hrow[:, q], 1.0, 0.0, ALU.mult, ALU.add, dots[q][:, i:i + 1])
                z.then_inc(dots_ready, 1)
            for s in range(2):
                gate(0, s)
                low(0, s)
                if s == 0:
                    rows_u(0, 0, first=True)
            with dve.Fori(1, NE // 2) as j:
                gate(j, 0)
                dve.wait_ge(y_added, j * YP)
                add(j - 1)
                low(j, 0)
                rows_v(j, 0)
                rows_u(j, 0)
                gate(j, 1)
                low(j, 1)
            dve.wait_ge(y_added, NE // 2 * YP)
            add(NE // 2 - 1)
            rows_v(NE // 2, 0)

        @block.tensor
        def _(pe):
            def hidden(j, s):
                e = j * 2 + s
                pe.wait_ge(u_hi_ready, e + 1)
                pe.wait_ge(u_lo_ready, e + 1)
                if not isinstance(j, int):
                    pe.wait_ge(act_done, e - 1)
                for b in range(NB):
                    cols = slice(b * TG, (b + 1) * TG)
                    for k in range(KD):
                        for i, (u, h) in enumerate(((u_hi, h_hi), (u_hi, h_lo), (u_lo, h_hi))):
                            mm = pe.matmul(g.ps[2 * s + b][:, 0:TG], u[s][:, k, :], h[:, k, cols],
                                           start=(k == 0 and i == 0), stop=(k == KD - 1 and i == 2))
                mm.then_inc(s_done, 1)

            def output(j):
                pe.wait_ge(a_lo_ready, j * 2 + 2)
                pe.wait_ge(v_lo_ready, j * 2 + 2)
                for m in range(YP):
                    pe.wait_ge(y_added, j * YP + (m - YB + 1 + YP if m >= YB else max(x for x in range(YP) if bank(x) == bank(m)) + 1))
                    rows, cols = slice((m // 2) * P, (m // 2 + 1) * P), slice((m % 2) * 512, (m % 2 + 1) * 512)
                    for s in range(2):
                        for i, (x, v) in enumerate(((a_hi, v_hi), (a_hi, v_lo), (a_lo, v_hi))):
                            mm = pe.matmul(g.ps[bank(m)][:], x[s][:, rows], v[s][:, cols],
                                           start=(s == 0 and i == 0), stop=(s == 1 and i == 2))
                    mm.then_inc(y_done, 1)
            pe.wait_ge(h_lo_ready, KD)
            hidden(0, 0)
            hidden(0, 1)
            with pe.Fori(1, NE // 2) as j:
                hidden(j, 0)
                output(j - 1)
                hidden(j, 1)
            output(NE // 2 - 1)


def final_norm(nc, g):
    with ExitStack() as ctx:
        sb = lambda n, s, d=F32: ctx.enter_context(nc.sbuf_tensor(n, s, d))
        sems = []
        sem = lambda n: new_sem(nc, ctx, f"fn_{n}", sems)
        x = sb("fnx", [P, NT, D])
        g2, lnf, junk = sb("g2", [P, 2, D]), sb("lnfw", [P, D]), sb("fnjunk", [P, D])
        ss = sb("fnss", [P, NT])
        small, loaded, chain, ms_ready, root_done, stored = (sem(n) for n in ("small", "ld", "chain", "ms", "root", "st"))
        ctx.callback(clear_sems, nc, sems)
        block = ctx.enter_context(nc.Block())

        @block.sync
        def _(sp):
            for dst, src in ((g2[:, 0], bcast_rows(g.mod_d[0, 5 * D:6 * D])), (g2[:, 1], bcast_rows(g.mod_d[1, 5 * D:6 * D])),
                             (lnf[:], bcast_rows(g.lnf)), (x[:], g.x1_d.rearrange("(t p) d -> p t d", p=P))):
                sp.dma_start(dst, src).then_inc(small, 16)
            with sp.Fori(0, NT) as t:
                sp.wait_ge(chain, t + (3 * NT + 2))
                sp.dma_start(g.y_all[bass.ds(t * P, P), :], x[:, bass.ds(t, 1), :].rearrange("p o d -> p (o d)")).then_inc(stored, 16)
            sp.wait_ge(stored, 16 * NT)

        @block.scalar
        def _(act):
            act.wait_ge(ms_ready, 1)
            act.activation(ss[:], ss[:], ACT.Sqrt).then_inc(root_done, 1)

        @block.vector
        def _(dve):
            own = Chain(dve, chain)
            dve.wait_ge(small, 64)
            for t in range(NT):
                seq = min(t, 1)
                own.link(dve.tensor_tensor(junk[:], g.Y[:, t], g2[:, seq], ALU.mult))
                own.link(dve.tensor_tensor(x[:, t], x[:, t], junk[:], ALU.add))
                own.link(dve.tensor_tensor_reduce(junk[:], x[:, t], x[:, t], 1.0 / D, EPS, ALU.mult, ALU.add, ss[:, t:t + 1]))
            dve.sem_inc(ms_ready, 1)
            dve.wait_ge(root_done, 1)
            own.link(dve.reciprocal(ss[:], ss[:]))
            for t in range(NT):
                own.link(dve.scalar_tensor_tensor(x[:, t], x[:, t], ss[:, t:t + 1], lnf[:], ALU.mult, ALU.mult))


def program(nc, g, ctx):
    sb = lambda n, s, d=F32: ctx.enter_context(nc.sbuf_tensor(n, s, d))
    g.ps = [ctx.enter_context(nc.psum_tensor(f"ps{i}", [P, 512], F32)) for i in range(8)]
    g.ident = sb("ident", [P, P])
    g.gain, g.shift = sb("gain", [P, 2, KD, 2]), sb("shift", [P, 2, KD, 2])
    with nc.sbuf_tensor("hT", [P, KD, T], F32) as g.hT:
        with nc.sbuf_tensor("X0", [P, NT, D], F32) as g.X:
            modulation(nc, g)
            norm_transpose(nc, g, 0)
        project_in(nc, g)
        with ExitStack() as mixer:
            sb = lambda n, s, d=F32: mixer.enter_context(nc.sbuf_tensor(n, s, d))
            g.DT, g.EC, g.WD, g.CD, g.NC = (sb(n, [P, NR, 16]) for n in ("DT", "EC", "WD", "CD", "NC"))
            g.sel, g.mneg = sb("sel", [16, 16, P]), sb("mneg", [P, 2, 4 * P])
            g.cumT, g.Dret = sb("cumT", [16, NR * P]), sb("Dret", [P, HEADS, P])
            g.SB, g.SBr = sb("SB", [P, NT + 1, W_]), sb("SBr", [HD, NT + 1, W_])
            decay_terms(nc, g)
            backward_states(nc, g)
            forward_scan(nc, g)
        with nc.sbuf_tensor("sel3", [P, 3, T], F32) as g.sel3:
            with nc.sbuf_tensor("wq", [P, KD, 2 * HEADS * P], F32) as g.wq:
                with nc.sbuf_tensor("X1", [P, NT, D], F32) as g.X:
                    norm_transpose(nc, g, 1)
                select_experts(nc, g)
            gather_inputs(nc, g)
            dense_gates(nc, g)
    with nc.sbuf_tensor("Y", [P, NT, D], F32) as g.Y:
        experts(nc, g)
        final_norm(nc, g)


def rope_tables():
    nf = HD // 4
    inv = np.float32(10000.0) ** (-np.arange(nf, dtype=np.float32) / np.float32(nf))
    t = np.arange(T - P)
    out = np.zeros((T, 2, 48), np.float32)
    out[:, :, 0:32] = 1.0
    for half, pos in enumerate((t // 64, t % 64)):
        ang = (pos.astype(np.float32)[:, None] * inv[None, :]).astype(np.float32)
        out[P:, half, 0:16] = out[P:, half, 16:32] = np.cos(ang.astype(np.float64))
        out[P:, half, 32:48] = np.sin(ang.astype(np.float64))
    return np.concatenate([out[:, :, 0:32].reshape(T, 64), out[:, :, 32:].reshape(T, 32)], 1)


def kernel(**inputs):
    import concourse.bacc as bacc
    from concourse.bass_utils import run_bass_kernel_spmd

    A = {k: np.asarray(v) for k, v in inputs.items()}
    f = np.ascontiguousarray
    rows = lambda a: f(np.broadcast_to(a, (P,) + a.shape))
    tok = np.arange(P)
    arrays = {
        "x_all": f(np.concatenate([A["x_prompt"][0], A["x_sample"][0]], 0)),
        "c_cols": f(np.stack([A["c_ctx"], A["c"][0]], 1).reshape(KD, P, 2).transpose(1, 0, 2)),
        "w_mod": A["w_mod"][0],
        "b_mod2": f(np.broadcast_to(A["b_mod"][0], (2, 6 * D))),
        "ln_cols": f(np.broadcast_to(np.stack([A["ln1_w"][0], A["ln2_w"][0]]).reshape(2, KD, P).transpose(2, 0, 1)[..., None],
                                     (P, 2, KD, 2))),
        "ident_d": np.eye(P, dtype=np.float32),
        "w_in": A["w_in"][0],
        "conv_w_cols": f(A["conv_w"][0].reshape(TAPS, XBC // P, P).transpose(2, 1, 0)),
        "conv_b_cols": f(A["conv_b"][0].reshape(XBC // P, P).T),
        "dt_biases": rows(np.concatenate([A["dt_bias_f"][0], A["dt_bias_b"][0]])),
        "a_logs": rows(np.concatenate([A["a_log_f"][0], A["a_log_b"][0]])),
        "ret_logits": rows(np.concatenate([A["ret_logit_f"][0], A["ret_logit_b"][0]])),
        "tri_d": f(np.stack([tok[:, None] <= tok[None], tok[:, None] >= tok[None], tok[:, None] >= 0 * tok[None]], 1).astype(np.float32)),
        "sel_d": f(np.broadcast_to(np.eye(16, dtype=np.float32)[:, :, None], (16, 16, P))),
        "mneg_d": f(np.tile(np.stack([np.where(tok[None] < tok[:, None], NEG, 0), np.where(tok[None] >= tok[:, None], NEG, 0)], 1)
                            .astype(np.float32), (1, 1, 4))),
        "rope_d": rope_tables(),
        "ssd_fwd_T": f(A["state_ssd_fwd"][0, 0].transpose(2, 0, 1).reshape(P, W_)),
        "ssd_bwd_T": f(A["state_ssd_bwd"][0, 0].transpose(2, 0, 1).reshape(P, W_)),
        "ret_fwd_T": f(A["state_ret_fwd"][0, 0].transpose(2, 0, 1).reshape(HD, W_)),
        "ret_bwd_T": f(A["state_ret_bwd"][0, 0].transpose(2, 0, 1).reshape(HD, W_)),
        "skip_row": f(np.repeat(A["d_skip"][0], HD)),
        "ssm_w": A["ssm_norm_w"][0],
        "gn_w": A["ret_gn_w"][0],
        "gn_b": A["ret_gn_b"][0],
        "w_out": A["w_out"][0],
        "peer_wq": A["peer_wq"][0],
        "keys_T": f(A["peer_keys"][0].reshape(2 * HEADS, NKEY, P).transpose(2, 0, 1)),
        "iota_d": f(np.broadcast_to(np.arange(P, dtype=np.float32), (P, P))),
        "u_T": f(A["peer_u"][0].reshape(NKEY, NKEY, KD, P).transpose(1, 3, 2, 0)),
        "peer_v": A["peer_v"][0].reshape(NKEY, NKEY, D),
        "u_rows": A["peer_u"][0],
        "lnf": A["lnf_w"],
    }
    nc = bacc.Bacc("TRN2", target_bir_lowering=False, num_devices=1)
    g = Ctx()
    for name, a in arrays.items():
        g.__dict__[name] = nc.dram_tensor(name, a.shape, mybir.dt.from_np(a.dtype), kind="ExternalInput").ap()
    scratch = {"mod_d": (2, 6 * D), "xbc_d": (XBC, T), "tok_d": (T, TC), "rec_d": (T, REC), "x1_d": (T, D),
               "h2T_d": (P, KD, T), "gates_d": (NKEY, P, TE), "rows_d": (P, GT, D), "pick_d": (P, 2, GT, NSEL)}
    for name, shape in scratch.items():
        g.__dict__[name] = nc.dram_tensor(name, shape, F32, kind="Internal").ap()
    g.v_rows = g.peer_v.rearrange("a b d -> (a b) d")
    outs = {"y_all": (T, D), "ssd_f_out": (P, W_), "ssd_b_out": (P, W_), "ret_f_out": (HD, W_), "ret_b_out": (HD, W_)}
    for name, shape in outs.items():
        g.__dict__[name] = nc.dram_tensor(name, shape, F32, kind="ExternalOutput").ap()
    with ExitStack() as ctx:
        program(nc, g, ctx)
    r = run_bass_kernel_spmd(nc, [arrays], core_ids=[0]).results[0]
    y = r["y_all"]
    turn = lambda a: f(a.reshape(-1, HEADS, HD).transpose(1, 2, 0)[None, None])
    return (f(y[None, :P]), f(y[None, P:]), turn(r["ssd_f_out"]), turn(r["ssd_b_out"]), turn(r["ret_f_out"]), turn(r["ret_b_out"]))
```
